# Optimizing a Trainium2 kernel written in Bass

```python
import math
import jax, jax.numpy as jnp
from jax import lax
import numpy as np

D_MODEL = 2048
BATCH = 1
SEQ = 256
DEPTH = 1

N_META = 16
BLK = 128
WINDOW = 128
HA = 8
DHA = 64
HBQ = 16
HBKV = 2
DHB = 64
G_B = HBQ // HBKV
D_FF = 4 * D_MODEL
N_BUCKETS = 32
MAX_DIST = 128
EPS = 1e-6
NEG = -1e30

QA_W = HA * 2 * DHA
KA_W = HA * 2 * DHA
VA_W = HA * 2 * DHA
QB_W = HBQ * DHB
KB_W = HBKV * DHB
VB_W = HBKV * DHB
WA = VA_W
WB = QB_W
IN_W = QA_W + KA_W + VA_W + QB_W + KB_W + VB_W + 2 * D_MODEL
SPLITS = list(np.cumsum([QA_W, KA_W, VA_W, QB_W, KB_W, VB_W, D_MODEL]).tolist())
PAD_FRONT = BLK - N_META

kernel_name = "hybrid_diffattn_swa_sink_gated_block"

def rmsnorm(x, g):
    xf = x.astype(jnp.float32)
    y = xf * lax.rsqrt(jnp.mean(xf * xf, axis=-1, keepdims=True) + EPS)
    return (y * g.astype(jnp.float32)).astype(x.dtype)

def t5_bucket(dist):
    n = jnp.maximum(dist, 0)
    max_exact = N_BUCKETS // 2
    nf = jnp.maximum(n, 1).astype(jnp.float32)
    large = max_exact + (jnp.log(nf / max_exact) / math.log(MAX_DIST / max_exact)
                         * (N_BUCKETS - max_exact)).astype(jnp.int32)
    large = jnp.minimum(large, N_BUCKETS - 1)
    return jnp.where(n < max_exact, n, large)

def diff_attention(q, k, v, rel_a, lam, lam_init, sub_g):
    B, P = q.shape[0], q.shape[1]
    nb = P // BLK
    pos = jnp.arange(P) - PAD_FRONT
    key_ok = pos >= 0
    qb = q.reshape(B, nb, BLK, HA, 2, DHA).transpose(1, 0, 2, 3, 4, 5)
    scale = DHA ** -0.5

    def one_block(args):
        q_blk, n = args
        qpos = n * BLK + jnp.arange(BLK) - PAD_FRONT
        dist = qpos[:, None] - pos[None, :]
        bias = rel_a[t5_bucket(dist)].astype(jnp.float32)
        mask = (dist >= 0) & key_ok[None, :]
        s = jnp.einsum('bqhcd,bkhcd->bhcqk', q_blk, k).astype(jnp.float32) * scale
        s = s + bias.transpose(2, 0, 1)[None, :, None]
        s = jnp.where(mask, s, NEG)
        p = jax.nn.softmax(s, axis=-1)
        a = p[:, :, 0] - lam * p[:, :, 1]
        return jnp.einsum('bhqk,bkhv->bqhv', a.astype(v.dtype), v)

    o = lax.map(one_block, (qb, jnp.arange(nb)))
    o = o.transpose(1, 0, 2, 3, 4).reshape(B, P, HA, 2 * DHA)
    o = rmsnorm(o, sub_g) * (1.0 - lam_init)
    return o.reshape(B, P, HA * 2 * DHA)

def swa_sink_attention(q, k, v, rel_b, sinks):
    B, P = q.shape[0], q.shape[1]
    nb = P // BLK
    scale = DHB ** -0.5
    qb = q.reshape(B, nb, BLK, HBKV, G_B, DHB)

    def band(t):
        tb = t.reshape(B, nb, BLK, HBKV, DHB)
        prev = jnp.concatenate([jnp.zeros_like(tb[:, :1]), tb[:, :-1]], axis=1)
        return jnp.concatenate([prev, tb], axis=2)

    kb, vb = band(k), band(v)
    km = k[:, PAD_FRONT:BLK]
    vm = v[:, PAD_FRONT:BLK]

    i = jnp.arange(BLK)
    j = jnp.arange(2 * BLK)
    m = jnp.arange(N_META)
    blocks = jnp.arange(nb)
    qpos = blocks[:, None] * BLK + i[None, :] - PAD_FRONT
    dist = BLK + i[:, None] - j[None, :]
    kidx = blocks[:, None] * BLK - BLK + j[None, :]
    band_mask = ((dist >= 0) & (dist < WINDOW))[None] & (kidx >= BLK)[:, None, :]
    dist_m = qpos[:, :, None] - m[None, None, :]
    meta_mask = dist_m >= 0

    bias_band = rel_b[t5_bucket(dist)].astype(jnp.float32)
    bias_band = bias_band.reshape(BLK, 2 * BLK, HBKV, G_B).transpose(2, 3, 0, 1)
    bias_meta = rel_b[t5_bucket(dist_m)].astype(jnp.float32)
    bias_meta = bias_meta.reshape(nb, BLK, N_META, HBKV, G_B).transpose(0, 3, 4, 1, 2)

    s_band = jnp.einsum('bnqhgd,bnkhd->bnhgqk', qb, kb).astype(jnp.float32) * scale + bias_band[None, None]
    s_band = jnp.where(band_mask[None, :, None, None], s_band, NEG)
    s_meta = jnp.einsum('bnqhgd,bmhd->bnhgqm', qb, km).astype(jnp.float32) * scale + bias_meta[None]
    s_meta = jnp.where(meta_mask[None, :, None, None], s_meta, NEG)
    sink = jnp.broadcast_to(sinks.astype(jnp.float32).reshape(HBKV, G_B)[None, None, :, :, None, None],
                            s_band.shape[:-1] + (1,))
    p = jax.nn.softmax(jnp.concatenate([s_meta, s_band, sink], axis=-1), axis=-1)
    p_meta = p[..., :N_META].astype(v.dtype)
    p_band = p[..., N_META:N_META + 2 * BLK].astype(v.dtype)
    o = (jnp.einsum('bnhgqm,bmhd->bnqhgd', p_meta, vm)
         + jnp.einsum('bnhgqk,bnkhd->bnqhgd', p_band, vb))
    return o.reshape(B, P, HBQ * DHB)

def setup_inputs(seed: int = 0) -> dict:
    key = jax.random.key(seed)
    ks = jax.random.split(key, 20)
    f32 = jnp.float32

    def nrm(k, shape, scale):
        return jax.random.normal(k, shape, f32) * scale

    def gain(k, shape):
        return 1.0 + 0.05 * jax.random.normal(k, shape, f32)

    return {
        "x": nrm(ks[0], (BATCH, SEQ, D_MODEL), 1.0),
        "meta_tokens": nrm(ks[1], (N_META, D_MODEL), 1.0),
        "rel_bias": nrm(ks[2], (N_BUCKETS, HA + HBQ), 0.5),
        "w_in": nrm(ks[3], (DEPTH, D_MODEL, IN_W), D_MODEL ** -0.5),
        "w_branch_a": nrm(ks[4], (DEPTH, WA, D_MODEL), WA ** -0.5),
        "w_branch_b": nrm(ks[5], (DEPTH, WB, D_MODEL), WB ** -0.5),
        "w_out": nrm(ks[6], (DEPTH, D_MODEL, D_MODEL), D_MODEL ** -0.5),
        "lambda_q1": nrm(ks[7], (DEPTH, DHA), 0.1),
        "lambda_k1": nrm(ks[8], (DEPTH, DHA), 0.1),
        "lambda_q2": nrm(ks[9], (DEPTH, DHA), 0.1),
        "lambda_k2": nrm(ks[10], (DEPTH, DHA), 0.1),
        "diff_norm": gain(ks[11], (DEPTH, 2 * DHA)),
        "sinks": nrm(ks[12], (DEPTH, HBQ), 1.0),
        "norm_attn_pre": gain(ks[13], (DEPTH, D_MODEL)),
        "norm_attn_post": gain(ks[14], (DEPTH, D_MODEL)),
        "w_ff1": nrm(ks[15], (DEPTH, D_MODEL, D_FF), D_MODEL ** -0.5),
        "w_ff2": nrm(ks[16], (DEPTH, D_FF, D_MODEL), D_FF ** -0.5),
        "norm_ff_pre": gain(ks[17], (DEPTH, D_MODEL)),
        "norm_ff_post": gain(ks[18], (DEPTH, D_MODEL)),
    }

def reference(x, meta_tokens, rel_bias, w_in, w_branch_a, w_branch_b, w_out,
              lambda_q1, lambda_k1, lambda_q2, lambda_k2, diff_norm, sinks,
              norm_attn_pre, norm_attn_post, w_ff1, w_ff2, norm_ff_pre, norm_ff_post):
    B = x.shape[0]
    pad = jnp.zeros((B, PAD_FRONT, D_MODEL), x.dtype)
    meta = jnp.broadcast_to(meta_tokens[None].astype(x.dtype), (B, N_META, D_MODEL))
    h = jnp.concatenate([pad, meta, x], axis=1)
    P = h.shape[1]
    rel_a = rel_bias[:, :HA]
    rel_b = rel_bias[:, HA:HA + HBQ]
    for l in range(DEPTH):
        lam_init = 0.8 - 0.6 * math.exp(-0.3 * l)
        lam = (jnp.exp(jnp.sum(lambda_q1[l].astype(jnp.float32) * lambda_k1[l].astype(jnp.float32)))
               - jnp.exp(jnp.sum(lambda_q2[l].astype(jnp.float32) * lambda_k2[l].astype(jnp.float32)))
               + lam_init)
        u = rmsnorm(h, norm_attn_pre[l])
        z = u @ w_in[l]
        qa, ka, va, qb, kb, vb, ga, gb = jnp.split(z, SPLITS, axis=-1)
        ya = diff_attention(qa.reshape(B, P, HA, 2, DHA), ka.reshape(B, P, HA, 2, DHA),
                            va.reshape(B, P, HA, 2 * DHA), rel_a, lam, lam_init, diff_norm[l])
        yb = swa_sink_attention(qb.reshape(B, P, HBQ, DHB), kb.reshape(B, P, HBKV, DHB),
                                vb.reshape(B, P, HBKV, DHB), rel_b, sinks[l])
        mix = jax.nn.sigmoid(ga) * (ya @ w_branch_a[l]) + jax.nn.sigmoid(gb) * (yb @ w_branch_b[l])
        h = h + rmsnorm(mix @ w_out[l], norm_attn_post[l])
        u = rmsnorm(h, norm_ff_pre[l])
        f = jnp.square(jax.nn.relu(u @ w_ff1[l])) @ w_ff2[l]
        h = h + rmsnorm(f, norm_ff_post[l])
    return h[:, BLK:]


_drawn_inputs = setup_inputs


def setup_inputs(seed=0):
    import zlib

    import numpy as np

    out = dict(_drawn_inputs(seed))
    spreads = {}
    factors = {'lambda_q2': 5.35, 'lambda_k2': 8.0, 'sinks': 8.0}
    for name, (base, spread) in spreads.items():
        noise = np.random.default_rng([zlib.crc32(name.encode()), seed]).standard_normal(out[name].shape)
        drawn = base * np.exp(spread * noise) if base else spread * noise
        out[name] = __import__('jax').numpy.asarray(drawn.astype(out[name].dtype))
    for name, factor in factors.items():
        out[name] = (out[name] * factor).astype(out[name].dtype)
    return out
```

```python
import math
from contextlib import ExitStack

import numpy as np

import concourse.bass as bass
from concourse import mybir

F32 = mybir.dt.float32
F32R = mybir.dt.float32r
ACT = mybir.ActivationFunctionType
ALU = mybir.AluOpType
AX = mybir.AxisListType

P = 128
D = 2048
SEQ = 256
BLOCKS = SEQ // P
META = 16
FF = 4 * D
HA, DHA = 8, 64
HB, HKV, DHB = 16, 2, 64
EPS = 1e-6
NEG = -1e30
LAM_INIT = 0.8 - 0.6 * math.exp(-0.3 * 0)
N_BUCKETS, MAX_DIST, WINDOW = 32, 128, 128

KT = D // P
CW = 512
UNITS = 8
UK = KT // UNITS
LEAD = 5
UT = 2 * META + SEQ

QA0, KA0, VA0 = 0, 1024, 2048
QB0, KB0, VB0 = 3072, 4096, 4224
GA0, GB0 = 4352, 6400

C_QB, C_A, C_GA, C_MIX, C_OUT, C_FF = 1, 3, 9, 13, 21, 25
N_MIX = D // CW
QUARTERS = 4

JOBS = HB // 2 + HA
START = [20 + 6 * j for j in range(HB // 2)] + [72 + 4 * j for j in range(HA)]
TURN_AT = {10: ("kvb", 0), 18: ("qb", 0), 31: ("qb", 1), 37: ("qa", 0), 43: ("ka", 0), 49: ("va", 0),
           61: ("qa", 1), 67: ("ka", 1), 74: ("va", 1)}
TURN_NO = {g: n for n, g in enumerate(TURN_AT.values())}

T_X, T_Y = 0, 9
T_M = T_Y + 8
T_H = T_M + 2 * N_MIX
T_F = T_H + 8

TAB = 400


def bucket_table():
    dist = np.arange(TAB) - 127
    n = np.maximum(dist, 0)
    exact = N_BUCKETS // 2
    nf = np.maximum(n, 1).astype(np.float32)
    large = exact + (np.log(nf / np.float32(exact)) / np.float32(math.log(MAX_DIST / exact))
                     * np.float32(N_BUCKETS - exact)).astype(np.int32)
    b = np.where(n < exact, n, np.minimum(large, N_BUCKETS - 1))
    out = np.zeros((N_BUCKETS + 1, 2, TAB), np.float32)
    for w, ok in enumerate((dist >= 0, (dist >= 0) & (dist < WINDOW))):
        out[b[ok], w, np.arange(TAB)[ok]] = 1.0
        out[N_BUCKETS, w, ~ok] = NEG
    return out


def hybrid_block(nc, x, meta_tokens, rel_bias, w_in, w_branch_a, w_branch_b, w_out, lambda_q1, lambda_k1,
                 lambda_q2, lambda_k2, diff_norm, sinks, norm_attn_pre, norm_attn_post, w_ff1, w_ff2,
                 norm_ff_pre, norm_ff_post, identity, fold, buckets, out):
    table = nc.dram_tensor("bias_table", (2, HA + HB, TAB), F32)

    ctx = ExitStack()
    with ctx:
        def sb(name, shape, dt=F32):
            return ctx.enter_context(nc.sbuf_tensor(name, shape, dt))

        def sem(name):
            return ctx.enter_context(nc.semaphore(name))

        def region(kb4, *groups):
            made = []
            for group in groups:
                with ExitStack() as g:
                    made.append([g.enter_context(nc.sbuf_tensor(*t)) for t in group])
            sb(f"keep_{groups[0][0][0]}", [P, kb4])
            return made

        (raw,), (w_lo,) = region(UNITS * UK * CW, [("raw", [P, UNITS, UK, CW], F32)],
                                 [("w_lo", [P, UNITS, UK, CW], F32R)])
        w_hi = sb("w_hi", [P, UNITS, UK, CW], F32R)

        (u_hi, u_lo), (h2, g_post, g_ffpre), (g_ffpost_keep, g_ffpost) = region(
            KT * (UT + SEQ),
            [("u_hi", [P, KT, UT], F32R), ("u_lo", [P, KT, SEQ], F32R)],
            [("h2", [P, BLOCKS, D], F32), ("g_post", [P, D], F32), ("g_ffpre", [P, D], F32)],
            [("g_ffpost_keep", [P, BLOCKS, D], F32), ("g_ffpost", [P, D], F32)])

        (qbT, kbT, vb, vb_m, qaT, kaT, va, va_m), (y_hi, y_lo), (f_hi, f_lo) = region(
            10400,
            [("qbT", [P, HB // 2, SEQ], F32), ("kbT", [P, HKV, 1 + META + SEQ], F32),
             ("vb", [P, BLOCKS, HKV * DHB], F32), ("vb_m", [META, HKV * DHB], F32),
             ("qaT", [P, HA, SEQ], F32), ("kaT", [P, HA, META + SEQ], F32),
             ("va", [P, BLOCKS, HA * P], F32), ("va_m", [META, HA * P], F32)],
            [("y_hi", [P, KT, SEQ], F32R), ("y_lo", [P, KT, SEQ], F32R)],
            [("f_hi", [P, KT, SEQ], F32R), ("f_lo", [P, KT, SEQ], F32R)])

        (y, t, pT, pTm, bias), (m_hi, m_lo), (hid_hi, hid_lo), (xs, xg) = region(
            2 * KT * SEQ,
            [("y", [P, BLOCKS, 2 * HA * P], F32), ("t", [P, 2, 418], F32), ("pT", [P, 2, 3 * P], F32),
             ("pTm", [META, 2, 2 * P], F32), ("bias", [P, 2, 2, 418], F32)],
            [("m_hi", [P, KT, SEQ], F32R), ("m_lo", [P, KT, SEQ], F32R)],
            [("hid_hi", [P, KT, SEQ], F32R), ("hid_lo", [P, KT, SEQ], F32R)],
            [("xs", [P, BLOCKS, D], F32), ("xg", [P, 8, CW], F32)])

        (ga,), (og,), (facc,), (xm, g_pre) = region(
            BLOCKS * D, [("ga", [P, BLOCKS, D], F32)], [("og", [P, BLOCKS, D], F32)],
            [("facc", [P, BLOCKS, D], F32)],
            [("xm", [2 * META, D], F32), ("g_pre", [P, D], F32)])

        rows = sb("rows", [P, BLOCKS, CW])
        rows_m = sb("rows_m", [2 * META, CW])
        gate_b = sb("gate_b", [P, BLOCKS, CW])
        ident = sb("ident", [P, P])
        fold_m = sb("fold_m", [2 * META, META])
        relx = sb("relx", [N_BUCKETS + 1, HA + HB])
        buck = sb("buck", [N_BUCKETS + 1, 2, TAB])
        lam_v = sb("lam_v", [P, 4, DHA])
        dcol = sb("dcol", [P, 1])
        sink_bc = sb("sink_bc", [P, HB])
        sc = sb("sc", [P, 96])
        eps = sc[:, 0:1]
        ssx, rstd, rstd8 = sc[:, 2:4], sc[:, 4:6], sc[:, 6:8]
        ssm, rstdm = sc[0:32, 8:9], sc[0:32, 9:10]
        lam_dot, lam_exp, neg_lam = sc[:, 10:12], sc[:, 12:14], sc[:, 14:15]
        mx, nmx, sums, rs, cc = sc[:, 16:20], sc[:, 20:24], sc[:, 24:28], sc[:, 28:32], sc[:, 32:34]
        ssy, rstdy = sc[:, 36:52], sc[:, 52:68]
        ss1, ss1t, rstd1 = sc[:, 68:76], sc[:, 76:78], sc[:, 78:80]
        ss2t, rstd2 = sc[:, 80:82], sc[:, 82:84]
        ss3t, rstd3 = sc[:, 84:86], sc[:, 86:88]
        ss2 = sb("ss2", [P, 8])
        ss3 = sb("ss3", [P, 8])

        bank = [ctx.enter_context(nc.psum_tensor(f"bank{i}", [P, 512], F32)) for i in range(8)]
        S0, S1, TB, MB = bank[4:8]

        x_landed = [sem(f"x_landed{i}") for i in range(2)]
        xm_landed, consts_landed = sem("xm_landed"), sem("consts_landed")
        rel_ones, rel_landed, small_landed = sem("rel_ones"), sem("rel_landed"), sem("small_landed")
        landed = [sem(f"landed{u}") for u in range(UNITS)]
        slot_free = sem("slot_free")
        hi_ready, lo_ready = sem("hi_ready"), sem("lo_ready")
        used = sem("used")
        acc_free = sem("acc_free")
        xg_ready = sem("xg_ready")
        turned, turned_hi, turned_lo = sem("turned"), sem("turned_hi"), sem("turned_lo")
        stats = sem("stats")
        norm = sem("norm")
        dve_seq = sem("dve_seq")
        table_ready, table_copied, table_stored = sem("table_ready"), sem("table_copied"), sem("table_stored")
        bias_landed = [sem(f"bias_landed{i}") for i in range(2)]
        sink_set, kb_zero = sem("sink_set"), sem("kb_zero")
        rows_ready, meta_ready = sem("rows_ready"), sem("meta_ready")
        proj_turned, proj_kept = sem("proj_turned"), sem("proj_kept")
        scores_ready, max_ready, exp_done, probs_ready = (sem("scores_ready"), sem("max_ready"),
                                                          sem("exp_done"), sem("probs_ready"))
        probs_turned, pT_kept, pTm_kept = sem("probs_turned"), sem("pT_kept"), sem("pTm_kept")
        o_ready, o_kept, ssy_ready = sem("o_ready"), sem("o_kept"), sem("ssy_ready")
        y_scaled = sem("y_scaled")
        gates_ready = sem("gates_ready")
        mix_part, mix_ready, a_free = sem("mix_part"), sem("mix_ready"), sem("a_free")
        tail_landed = sem("tail_landed")
        o_squared, hg_part, hg_ready = sem("o_squared"), sem("hg_part"), sem("hg_ready")
        facc_zero, relu_ready, act_ready = sem("facc_zero"), sem("relu_ready"), sem("act_ready")
        g2_landed, f_squared, out_ready, stored = (sem("g2_landed"), sem("f_squared"),
                                                            sem("out_ready"), sem("stored"))

        xf = x[0].rearrange("(b p) d -> p b d", p=P)
        outf = out[0].rearrange("(b p) d -> p b d", p=P)

        def unit_of(w, krange, nrange):
            return w[0, krange, nrange].rearrange("(k p) n -> p k n", p=P)

        def w_in_column(c):
            if c == 0:
                return KB0
            if c < C_A:
                return QB0 + (c - C_QB) * CW
            if c < C_GA:
                i, kind = divmod(c - C_A, 3)
                return (QA0, KA0, VA0)[kind] + i * CW
            return GA0 + (c - C_GA) * CW

        def bcast(v, n=P):
            return v.partition_broadcast(n)

        block = ctx.enter_context(nc.Block())

        @block.sync
        def _(sp):
            half = D // 2
            for i in range(2):
                cols = slice(i * half, (i + 1) * half)
                sp.dma_start(g_pre[:, cols], bcast(norm_attn_pre[0, cols])).then_inc(x_landed[i], 16)
                sp.dma_start(xs[:, :, cols], xf[:, :, cols]).then_inc(x_landed[i], 16)

            def load(u, w, krange, nrange, free, width=CW):
                if free is not None:
                    sp.wait_ge(used, free)
                    sp.sem_inc(slot_free, 1)
                sp.dma_start(raw[:, u, :, 0:width], unit_of(w, krange, nrange)).then_inc(landed[u], 16)

            for c in range(C_MIX):
                width = 256 if c == 0 else CW
                n0 = w_in_column(c)
                for u in range(UNITS):
                    load(u, w_in, slice(u * 256, u * 256 + 256), slice(n0, n0 + width),
                         8 * c + u - 7 if c else None, width)
            with sp.Fori(0, N_MIX) as n:
                for u in range(UNITS):
                    load(u, w_in, slice(u * 256, u * 256 + 256), bass.ds(GB0 + n * CW, CW),
                         8 * C_MIX + u - 7 + n * 16)
                for u in range(UNITS):
                    w = w_branch_b if u < 4 else w_branch_a
                    k0 = (u % 4) * 256
                    load(u, w, slice(k0, k0 + 256), bass.ds(n * CW, CW), 8 * C_MIX + 8 + u - 7 + n * 16)
            with sp.Fori(0, N_MIX) as n:
                for u in range(UNITS):
                    load(u, w_out, slice(u * 256, u * 256 + 256), bass.ds(n * CW, CW),
                         8 * C_OUT + u - 7 + n * 8)
            with sp.Fori(0, QUARTERS) as q:
                for j in range(4):
                    for u in range(UNITS):
                        load(u, w_ff1, slice(u * 256, u * 256 + 256), bass.ds(q * D + j * CW, CW),
                             8 * (C_FF + j) + u - 7 + q * 64)
                for j in range(4):
                    for u in range(UNITS):
                        load(u, w_ff2, bass.ds(q * D + u * 256, 256), slice(j * CW, j * CW + CW),
                             8 * (C_FF + 4 + j) + u - 7 + q * 64)
            for b in range(BLOCKS):
                sp.wait_ge(out_ready, b + 1)
                sp.dma_start(outf[:, b, :], facc[:, b, :]).then_inc(stored, 16)
            sp.wait_ge(stored, 16 * BLOCKS)

        @block.gpsimd
        def _(pool):
            pool.memset(relx[:], 1.0).then_inc(rel_ones, 1)
            pool.memset(kbT[:, :, 0:1], 0.0).then_inc(kb_zero, 1)
            for i, v in enumerate((lambda_q1, lambda_k1, lambda_q2, lambda_k2)):
                pool.dma_start(lam_v[:, i, :], bcast(v[0])).then_inc(small_landed, 16)
            pool.dma_start(dcol[:], diff_norm[0].rearrange("(p a) -> p a", a=1)).then_inc(small_landed, 16)
            pool.dma_start(sink_bc[:], bcast(sinks[0])).then_inc(small_landed, 16)
            pool.dma_start(fold_m[:], fold).then_inc(small_landed, 16)

            def job_bias(j):
                slot = j % 2
                if j >= 2:
                    pool.wait_ge(max_ready, j - 1)
                if j < HB // 2:
                    row = HA + 2 * j
                    for w, t0, at, n in ((1, 0, 0, 128), (0, 128, 128, META), (1, 0, 145, 256),
                                         (0, 256, 401, META)):
                        src = bass.AP(table, (w * (HA + HB) + row) * TAB + t0, [[1, P], [TAB, 2], [1, n]])
                        pool.dma_start(bias[:, slot, :, at:at + n], src).then_inc(bias_landed[slot], 16)
                    v = bias[:, slot, :, :]
                    for e in range(2):
                        for at in (144, 417):
                            last = pool.tensor_copy(v[:, e, at:at + 1], sink_bc[:, 2 * j + e:2 * j + e + 1])
                    last.then_inc(sink_set, 1)
                else:
                    src = bass.AP(table, (j - HB // 2) * TAB, [[1, P], [1, META + SEQ]])
                    pool.dma_start(bias[:, slot, 0, 0:META + SEQ], src).then_inc(bias_landed[slot], 16)

            pool.wait_ge(small_landed, 7 * 16)
            pool.wait_ge(table_copied, 1)
            pool.dma_start(table.ap().rearrange("w h t -> h w t"), rows[0:HA + HB, :, 0:TAB])\
                .then_inc(table_stored, 16)
            pool.wait_ge(table_stored, 16)
            pool.wait_ge(turned, T_Y)
            for j in range(JOBS):
                job_bias(j)
            pool.wait_ge(norm, 5)
            pool.memset(facc[:], 0.0).then_inc(facc_zero, 1)

        @block.scalar
        def _(act):
            def split_hi(u, chunk, width=CW):
                act.wait_ge(landed[u], 16 + 16 * chunk)
                act.activation(w_hi[:, u, :, 0:width], raw[:, u, :, 0:width], ACT.Copy).then_inc(hi_ready, 1)

            def split_ahead(c, u):
                uu = (u + LEAD) % UNITS
                split_hi(uu, c + (u + LEAD) // UNITS)

            def keep_hi(n, dst, src, scale=None):
                act.wait_ge(turned, n + 1)
                if scale is None:
                    act.activation(dst, src, ACT.Copy).then_inc(turned_hi, 1)
                else:
                    act.activation(dst, src, ACT.Identity, scale=scale).then_inc(turned_hi, 1)

            act.dma_start(ident[:], identity).then_inc(consts_landed, 16)
            act.dma_start(xm[0:META, :], meta_tokens).then_inc(xm_landed, 16)
            act.dma_start(xm[META:2 * META, :], meta_tokens).then_inc(xm_landed, 16)
            act.dma_start(buck[:], buckets).then_inc(consts_landed, 16)
            act.wait_ge(rel_ones, 1)
            act.dma_start(relx[0:N_BUCKETS, :], rel_bias).then_inc(rel_landed, 16)

            for i in range(8):
                j, b = divmod(i, 2)
                keep_hi(i, u_hi[:, 4 * j:4 * j + 4, 2 * META + b * P:2 * META + (b + 1) * P],
                        bank[i][:].rearrange("p (k t) -> p k t", k=4))
                if i >= 3:
                    split_hi(i - 3, 0, 256)
            act.wait_ge(turned, 9)
            mt = bank[0][:].rearrange("p (k t) -> p k t", t=2 * META)
            act.activation(u_hi[:, :, 0:META], mt[:, :, 0:META], ACT.Copy).then_inc(turned_hi, 1)
            for b in range(BLOCKS):
                for j in range(4):
                    if b or j:
                        act.wait_ge(stats, b * 4 + j)
                    act.activation(gate_b[:, 0, :], xs[:, b, j * CW:(j + 1) * CW], ACT.Square,
                                   accum_out=ss3[:, b * 4 + j:b * 4 + j + 1]).then_inc(stats, 1)
            act.wait_ge(norm, 1)
            act.activation(rstd, ssx, ACT.Sqrt, scale=1.0 / D, bias=eps).then_inc(stats, 1)
            act.activation(rstdm, ssm, ACT.Sqrt, scale=1.0 / D, bias=eps[0:32, :]).then_inc(stats, 1)
            act.wait_ge(norm, 2)
            act.activation(lam_exp, lam_dot, ACT.Exp).then_inc(stats, 1)

            def keep_meta(c):
                act.wait_ge(used, 8 * (c + 1))
                if c == 0:
                    act.wait_ge(norm, 3)
                    dup = MB[0:32, 0:P].rearrange("p (g a d) -> p g a d", g=HKV, a=1)\
                        .broadcast_to([32, HKV, 2, DHB])
                    act.activation(rows_m[:, 0:2 * P].rearrange("p (g a d) -> p g a d", g=HKV, a=2), dup,
                                   ACT.Identity, scale=rstdm)
                    act.activation(rows_m[:, 2 * P:3 * P], MB[0:32, P:2 * P], ACT.Identity, scale=rstdm)\
                       .then_inc(meta_ready, 1)
                    return
                act.wait_ge(proj_turned, meta_done[c])
                act.activation(rows_m[:], MB[0:32, :], ACT.Identity, scale=rstdm).then_inc(meta_ready, 1)

            meta_done = {4: 1, 5: TURN_NO[("ka", 0)] + 1, 7: TURN_NO[("va", 0)] + 1, 8: TURN_NO[("ka", 1)] + 1}

            def keep_chunk(c):
                ps = [bank[2 * (c % 2) + b] for b in range(BLOCKS)]
                act.wait_ge(used, 8 * (c + 1))
                if c == 0:
                    act.wait_ge(table_stored, 16)
                    for b in range(BLOCKS):
                        dup = ps[b][:, 0:128].rearrange("p (g a d) -> p g a d", g=HKV, a=1)\
                            .broadcast_to([P, HKV, 2, DHB])
                        act.activation(rows[:, b, 0:256].rearrange("p (g a d) -> p g a d", g=HKV, a=2), dup,
                                       ACT.Identity, scale=rstd[:, b:b + 1])
                        act.activation(vb[:, b, :], ps[b][:, 128:256], ACT.Identity,
                                       scale=rstd[:, b:b + 1]).then_inc(acc_free, 1)
                elif c < C_A or (c < C_GA and (c - C_A) % 3 < 2):
                    is_q = c < C_A or (c - C_A) % 3 == 0
                    act.wait_ge(proj_turned, rows_done[c])
                    for b in range(BLOCKS):
                        act.activation(rows[:, b, :], ps[b][:], ACT.Identity,
                                       scale=(rstd8 if is_q else rstd)[:, b:b + 1]).then_inc(acc_free, 1)
                elif c < C_GA:
                    i = (c - C_A) // 3
                    for b in range(BLOCKS):
                        act.activation(va[:, b, i * CW:(i + 1) * CW], ps[b][:], ACT.Identity,
                                       scale=rstd[:, b:b + 1]).then_inc(acc_free, 1)
                else:
                    i = c - C_GA
                    for b in range(BLOCKS):
                        act.activation(ga[:, b, i * CW:(i + 1) * CW], ps[b][:], ACT.Identity,
                                       scale=rstd[:, b:b + 1]).then_inc(acc_free, 1)

            rows_done = {1: 1, 2: 2, 3: 3, 4: 4, 6: 5, 7: 7}

            def job_exp(j):
                s0 = 1 if j < HB // 2 else 0
                n0 = P + META + s0
                act.wait_ge(max_ready, j + 1)
                for e in range(2):
                    for q, (a, b) in enumerate(((0, n0), (n0, 2 * n0 + P))):
                        last = act.activation(t[:, e, a:b], t[:, e, a:b], ACT.Exp,
                                              bias=nmx[:, 2 * e + q:2 * e + q + 1],
                                              accum_out=sums[:, 2 * e + q:2 * e + q + 1])
                last.then_inc(exp_done, 1)

            def job_keep_probs(j):
                act.wait_ge(probs_turned, j + 1)
                for e, src in enumerate((TB, S0) if j < HB // 2 else (TB,)):
                    act.activation(pTm[:, e, 0:P], src[0:META, 3 * P:4 * P], ACT.Copy)
                    last = act.activation(pT[:, e, :], src[:, 0:3 * P], ACT.Copy)
                last.then_inc(pT_kept, 1)

            def job_squares(j):
                h = j - HB // 2
                act.wait_ge(o_kept, j + 1)
                if h:
                    act.wait_ge(ssy_ready, 2 * h)
                for b in range(BLOCKS):
                    act.activation(gate_b[:, b, 0:P], y[:, b, h * P:(h + 1) * P], ACT.Square,
                                   accum_out=ssy[:, b * HA + h:b * HA + h + 1]).then_inc(ssy_ready, 1)

            def attention(tau):
                for j in range(JOBS):
                    if tau == START[j] + 1:
                        job_exp(j)
                    if tau == START[j] + 4:
                        job_keep_probs(j)
                    if tau == START[j] + 6 and j >= HB // 2:
                        job_squares(j)

            for c in range(C_MIX):
                for u in range(UNITS):
                    tau = 8 * c + u
                    if u == 0 and c >= 1 and has_meta(c - 1):
                        keep_meta(c - 1)
                    if u == 1 and c >= 1:
                        keep_chunk(c - 1)
                    attention(tau)
                    split_ahead(c, u) if tau + LEAD >= 8 else split_hi(tau + LEAD, 0, 256)

            def gates(n, sl):
                act.wait_ge(acc_free, 2 * C_MIX)
                for b in range(BLOCKS):
                    act.activation(ga[:, b, sl], ga[:, b, sl], ACT.Sigmoid).then_inc(gates_ready, 1)

            def gate_b_sigmoid(n, c):
                act.wait_ge(used, 8 + 8 * c)
                for b in range(BLOCKS):
                    act.activation(gate_b[:, b, :], bank[2 + b][:], ACT.Sigmoid,
                                   scale=rstd[:, b:b + 1]).then_inc(acc_free, 1)

            def keep_mix(n):
                for g in range(2):
                    keep_hi(T_M + 2 * n + g, m_hi[:, bass.ds(4 * n + 2 * g, 2), :],
                            bank[4 + g][:].rearrange("p (k t) -> p k t", k=2))

            def mix_pair(n, first):
                cg = C_MIX + 2 * n
                for u in range(UNITS):
                    if first:
                        if u == 1:
                            keep_chunk(C_MIX - 1)
                        attention(8 * C_MIX + u)
                        if u == 3:
                            act.wait_ge(ssy_ready, 2 * HA)
                            act.activation(rstdy, ssy, ACT.Sqrt, scale=1.0 / P, bias=eps)\
                               .then_inc(stats, 1)
                        if u >= 1:
                            keep_y(u - 1)
                    elif u == 4:
                        keep_mix(n - 1)
                    if u == 6:
                        gates(n, bass.ds(n * CW, CW))
                    split_ahead(cg, u)
                for u in range(UNITS):
                    if first and u == 0:
                        keep_y(7)
                    if u == 1:
                        gate_b_sigmoid(n, cg)
                    split_ahead(cg + 1, u)

            def keep_y(i):
                g = (i + 4) % 8
                keep_hi(T_Y + i, y_hi[:, 2 * g:2 * g + 2, :],
                        bank[4 + i % 2][:].rearrange("p (k t) -> p k t", k=2), dcol[:] if g < 4 else None)

            mix_pair(0, True)
            with act.Fori(1, N_MIX) as n:
                mix_pair(n, False)

            def square_out(j):
                act.wait_ge(used, 8 * (C_OUT + j + 1))
                ps = [bank[2 * ((C_OUT + j) % 2) + b] for b in range(BLOCKS)]
                if j:
                    act.wait_ge(o_squared, 2 * j)
                for b in range(BLOCKS):
                    act.activation(gate_b[:, b, :], ps[b][:], ACT.Square,
                                   accum_out=ss1[:, b * 4 + j:b * 4 + j + 1]).then_inc(o_squared, 1)

            act.wait_ge(used, 8 * (C_OUT - 1))
            act.dma_start(g_post[:], bcast(norm_attn_post[0])).then_inc(tail_landed, 16)
            act.dma_start(h2[:], xf).then_inc(tail_landed, 16)
            act.dma_start(g_ffpre[:], bcast(norm_ff_pre[0])).then_inc(tail_landed, 16)
            for j in range(4):
                for u in range(UNITS):
                    if j == 0 and u == 4:
                        keep_mix(N_MIX - 1)
                    if j >= 1 and u == 1:
                        square_out(j - 1)
                    split_ahead(C_OUT + j, u)
            square_out(3)
            act.wait_ge(norm, 4)
            act.activation(rstd1, ss1t, ACT.Sqrt, scale=1.0 / D, bias=eps).then_inc(stats, 1)

            def square_h2(j):
                for b in range(BLOCKS):
                    act.activation(og[:, b, j * CW:(j + 1) * CW], h2[:, b, j * CW:(j + 1) * CW], ACT.Square,
                                   accum_out=ss2[:, b * 4 + j:b * 4 + j + 1]).then_inc(stats, 1)

            for j in range(4):
                for g in range(2):
                    keep_hi(T_H + 2 * j + g, f_hi[:, 4 * j + 2 * g:4 * j + 2 * g + 2, :],
                            bank[4 + 2 * (j % 2) + g][:].rearrange("p (k t) -> p k t", k=2))
                square_h2(j)
            act.wait_ge(norm, 5)
            act.activation(rstd2, ss2t, ACT.Sqrt, scale=1.0 / D, bias=eps).then_inc(stats, 1)

            def relu_rows(q, j):
                ps = [bank[2 * ((C_FF + j) % 2) + b] for b in range(BLOCKS)]
                act.wait_ge(used, 8 * (C_FF + j + 1) + q * 64)
                act.wait_ge(turned, T_F + 2 * j + q * 8)
                for b in range(BLOCKS):
                    act.activation(rows[:, b, :], ps[b][:], ACT.Relu, scale=rstd2[:, b:b + 1])\
                       .then_inc(acc_free, 1)

            def keep_hidden(q, j):
                for g in range(2):
                    keep_hi(T_F + 2 * j + g + q * 8, hid_hi[:, 4 * j + 2 * g:4 * j + 2 * g + 2, :],
                            bank[4 + 2 * (j % 2) + g][:].rearrange("p (k t) -> p k t", k=2))

            def quarter(q, last):
                for j in range(8):
                    for u in range(UNITS):
                        if 1 <= j <= 4 and u == 1:
                            relu_rows(q, j - 1)
                        if 1 <= j <= 4 and u == 4:
                            keep_hidden(q, j - 1)
                        if last and j >= 5 and u == 2:
                            square_f(j - 5)
                        if not (last and j == 7 and u + LEAD >= UNITS):
                            uu = (u + LEAD) % UNITS
                            split_hi(uu, C_FF + j + (u + LEAD) // UNITS + q * 8)

            def square_f(j):
                if j:
                    act.wait_ge(f_squared, 2 * j)
                for b in range(BLOCKS):
                    act.wait_ge(acc_free, 2 * (C_FF + 8 * 3 + 4 + j) + b + 1)
                    act.activation(gate_b[:, b, :], facc[:, b, j * CW:(j + 1) * CW], ACT.Square,
                                   accum_out=ss3[:, b * 4 + j:b * 4 + j + 1]).then_inc(f_squared, 1)

            act.dma_start(g_ffpost[:], bcast(norm_ff_post[0])).then_inc(g2_landed, 16)
            act.wait_ge(norm, 6)
            with act.Fori(0, QUARTERS - 1) as q:
                quarter(q, False)
            quarter(QUARTERS - 1, True)
            square_f(3)
            act.wait_ge(norm, 7)
            act.activation(rstd3, ss3t, ACT.Sqrt, scale=1.0 / D, bias=eps).then_inc(stats, 1)

        @block.vector
        def _(dve):
            seq = [0]

            def link(ins):
                seq[0] += 1
                ins.then_inc(dve_seq, 1)
                dve.wait_ge(dve_seq, seq[0])

            def split_lo(u, count, width=CW):
                dve.wait_ge(hi_ready, count)
                dve.tensor_tensor(w_lo[:, u, :, 0:width], raw[:, u, :, 0:width],
                                  w_hi[:, u, :, 0:width].bitcast(F32), ALU.subtract).then_inc(lo_ready, 1)

            def split_ahead(c8, u):
                split_lo((u + LEAD) % UNITS, c8 + (u + LEAD + 1))

            def keep_lo(n, dst, src, hi, scale=None):
                dve.wait_ge(turned_hi, n + 1)
                if scale is None:
                    dve.tensor_tensor(dst, src, hi.bitcast(F32), ALU.subtract).then_inc(turned_lo, 1)
                else:
                    dve.scalar_tensor_tensor(dst, src, scale, hi.bitcast(F32), ALU.mult, ALU.subtract)\
                       .then_inc(turned_lo, 1)

            def x_times_gain(i):
                j, b = divmod(i, 2)
                if i % 4 == 0:
                    dve.wait_ge(x_landed[i // 4], 32)
                cols = slice(j * CW, (j + 1) * CW)
                dve.tensor_tensor(xg[:, i, :], xs[:, b, cols], g_pre[:, cols], ALU.mult).then_inc(xg_ready, 1)

            def keep_x(i):
                j, b = divmod(i, 2)
                keep_lo(i, u_lo[:, 4 * j:4 * j + 4, b * P:(b + 1) * P],
                        bank[i][:].rearrange("p (k t) -> p k t", k=4),
                        u_hi[:, 4 * j:4 * j + 4, 2 * META + b * P:2 * META + (b + 1) * P])

            dve.memset(eps, EPS)
            for i in range(4):
                x_times_gain(i)
            for i in range(4):
                keep_x(i)
                x_times_gain(4 + i)
            dve.wait_ge(xm_landed, 32)
            for j in range(4):
                cols = slice(j * CW, (j + 1) * CW)
                link(dve.tensor_tensor_reduce(rows_m[:], xm[:, cols], xm[:, cols], 1.0, 0.0, ALU.mult, ALU.add,
                                              ss1[0:32, j:j + 1]))
            link(dve.tensor_reduce(ssm, ss1[0:32, 0:4], AX.X, ALU.add))
            dve.tensor_tensor(xm[:], xm[:], g_pre[0:32, :], ALU.mult).then_inc(xg_ready, 1)
            for i in range(4, 8):
                keep_x(i)
            mt = bank[0][:].rearrange("p (k t) -> p k t", t=2 * META)
            dve.wait_ge(turned_hi, 9)
            dve.tensor_tensor(u_hi[:, :, META:2 * META], mt[:, :, META:2 * META],
                              u_hi[:, :, 0:META].bitcast(F32), ALU.subtract).then_inc(turned_lo, 1)
            for u in range(LEAD):
                split_lo(u, u + 1, 256)
            dve.wait_ge(table_ready, 1)
            for w in range(2):
                last = dve.tensor_copy(rows[0:HA + HB, w, 0:TAB], bank[1 + w][0:HA + HB, 0:TAB])
            last.then_inc(table_copied, 1)
            dve.wait_ge(stats, 8)
            dve.tensor_reduce(ssx, ss3[:].rearrange("p (b j) -> p b j", b=BLOCKS), AX.X, ALU.add)\
               .then_inc(norm, 1)
            dve.wait_ge(small_landed, 7 * 16)
            for i in range(2):
                last = dve.tensor_tensor_reduce(lam_v[:, 2 * i, :], lam_v[:, 2 * i, :], lam_v[:, 2 * i + 1, :],
                                                1.0, 0.0, ALU.mult, ALU.add, lam_dot[:, i:i + 1])
            last.then_inc(norm, 1)
            dve.wait_ge(stats, 10)
            link(dve.reciprocal(rstd, rstd))
            link(dve.reciprocal(rstdm, rstdm))
            dve.tensor_scalar(rstd8, rstd, DHA ** -0.5, None, ALU.mult).then_inc(norm, 1)
            dve.wait_ge(stats, 11)
            link(dve.scalar_tensor_tensor(neg_lam, lam_exp[:, 1:2], LAM_INIT, lam_exp[:, 0:1], ALU.subtract,
                                          ALU.subtract))
            link(dve.tensor_scalar(dcol[:], dcol[:], 1.0 - LAM_INIT, None, ALU.mult))

            def keep_turned(kind, i):
                n = TURN_NO[(kind, i)]
                dve.wait_ge(proj_turned, n + 1)
                g2 = [S0[:].rearrange("p (k t) -> p k t", k=2), TB[:].rearrange("p (k t) -> p k t", k=2)]
                if kind == "kvb":
                    dve.tensor_copy(kbT[:, :, 1 + META:], g2[0])
                    dve.tensor_copy(kbT[:, :, 1:1 + META],
                                    S1[:, 0:2 * META].rearrange("p (k t) -> p k t", k=2))
                    last = dve.tensor_copy(vb_m[:], S1[0:META, 64:64 + P])
                elif kind == "va":
                    last = dve.tensor_copy(va_m[:, i * CW:(i + 1) * CW], TB[0:META, :])
                else:
                    dst, off = {"qb": (qbT, 0), "qa": (qaT, 0), "ka": (kaT, META)}[kind]
                    if kind == "ka":
                        dve.tensor_copy(kaT[:, 4 * i:4 * i + 4, 0:META],
                                        S1[:, 0:4 * META].rearrange("p (k t) -> p k t", k=4))
                    for g in range(2):
                        k0 = 4 * i + 2 * g
                        last = dve.tensor_copy(dst[:, k0:k0 + 2, off:off + SEQ], g2[g])
                last.then_inc(proj_kept, 1)

            def reverse(v, lo, n):
                return v[:, lo + n - 1:(lo - 1 if lo else None):-1]

            def job_max(j):
                windowed = j < HB // 2
                s0 = 1 if windowed else 0
                n0 = P + META + s0
                slot = j % 2
                dve.wait_ge(scores_ready, j + 1)
                if windowed:
                    dve.wait_ge(bias_landed[slot], 64 * (j // 2 + 1))
                    dve.wait_ge(sink_set, j + 1)
                else:
                    dve.wait_ge(bias_landed[slot], 64 * 4 + 16 * ((j - 8) // 2 + 1))
                for e, S in enumerate((S0, S1)):
                    for q, (a, n) in enumerate(((0, n0), (n0, n0 + P))):
                        bv = bias[:, slot, e if windowed else 0, :]
                        lo = a if windowed else 0
                        last = dve.tensor_tensor_reduce(t[:, e, a:a + n], S[:, a:a + n], reverse(bv, lo, n), 1.0,
                                                        -3.0e38, ALU.add, ALU.max,
                                                        mx[:, 2 * e + q:2 * e + q + 1])
                link(last)
                dve.tensor_scalar(nmx, mx, -1.0, None, ALU.mult).then_inc(max_ready, 1)

            def job_combine(j):
                dve.wait_ge(exp_done, j + 1)
                if j < HB // 2:
                    dve.reciprocal(rs, sums).then_inc(probs_ready, 1)
                    return
                link(dve.reciprocal(rs, sums))
                link(dve.scalar_tensor_tensor(cc, sums[:, 0:2], neg_lam, rs[:, 2:4], ALU.mult, ALU.mult))
                n0 = P + META
                for q, (a, n) in enumerate(((0, n0), (n0, n0 + P))):
                    last = dve.scalar_tensor_tensor(t[:, 0, a:a + n], t[:, 1, a:a + n], cc[:, q:q + 1],
                                                    t[:, 0, a:a + n], ALU.mult, ALU.add)
                last.then_inc(probs_ready, 1)

            def job_keep_meta_probs(j):
                dve.wait_ge(probs_turned, j + 1)
                if j < HB // 2:
                    dve.tensor_copy(pTm[:, :, P:2 * P], S1[0:META, 0:2 * P].rearrange("p (e t) -> p e t", e=2))\
                       .then_inc(pTm_kept, 1)
                else:
                    dve.tensor_copy(pTm[:, 0, P:2 * P], MB[0:META, 0:P]).then_inc(pTm_kept, 1)

            def job_keep_out(j):
                dve.wait_ge(o_ready, j + 1)
                if j < HB // 2:
                    c0 = HA * P + j * P
                    dst = y[:, :, c0:c0 + P].rearrange("p q (e d) -> p q e d", e=2)
                    src = S1[:, 2 * P:4 * P].rearrange("p (q e d) -> p q e d", q=2, e=2)
                    r = rs.rearrange("p (e q a) -> p q e a", e=2, a=1).broadcast_to([P, 2, 2, DHB])
                else:
                    h = j - HB // 2
                    dst = y[:, :, h * P:(h + 1) * P]
                    src = MB[:, P:3 * P].rearrange("p (q d) -> p q d", q=2)
                    r = rs[:, 0:2].rearrange("p (q a) -> p q a", a=1).broadcast_to([P, 2, P])
                dve.tensor_tensor(dst, src, r, ALU.mult).then_inc(o_kept, 1)

            def attention(tau):
                for j in range(JOBS):
                    if tau == START[j] + 5:
                        job_keep_out(j)
                    if tau == START[j] + 1:
                        job_max(j)
                    if tau == START[j] + 2:
                        job_combine(j)
                    if tau == START[j] + 4:
                        job_keep_meta_probs(j)
                if tau - 1 in TURN_AT:
                    keep_turned(*TURN_AT[tau - 1])

            for c in range(C_MIX):
                for u in range(UNITS):
                    tau = 8 * c + u
                    attention(tau)
                    if tau + LEAD < 8:
                        split_lo(tau + LEAD, tau + LEAD + 1, 256)
                    else:
                        split_ahead(8 * c, u)

            def keep_y(i):
                g = (i + 4) % 8
                keep_lo(T_Y + i, y_lo[:, 2 * g:2 * g + 2, :],
                        bank[4 + i % 2][:].rearrange("p (k t) -> p k t", k=2), y_hi[:, 2 * g:2 * g + 2, :],
                        dcol[:] if g < 4 else None)

            def mix_b(n):
                dve.wait_ge(used, 8 * (C_MIX + 1) + 4 + n * 16)
                dve.wait_ge(acc_free, 2 * (C_MIX + 1) + n * 4)
                for b in range(BLOCKS):
                    dve.tensor_tensor(gate_b[:, b, :], bank[b][:], gate_b[:, b, :], ALU.mult)\
                       .then_inc(acc_free, 1)

            def mix_a(n):
                dve.wait_ge(used, 8 * (C_MIX + 2) + n * 16)
                dve.wait_ge(gates_ready, 2 + n * 2)
                for b in range(BLOCKS):
                    dve.tensor_tensor(rows[:, b, :], bank[6 + b][:], ga[:, b, bass.ds(n * CW, CW)], ALU.mult)\
                       .then_inc(mix_part, 1)
                for b in range(BLOCKS):
                    dve.wait_ge(mix_part, n * 2 + b + 1)
                    dve.tensor_tensor(rows[:, b, :], rows[:, b, :], gate_b[:, b, :], ALU.add)\
                       .then_inc(mix_ready, 1)

            def keep_mix(n):
                for g in range(2):
                    sl = bass.ds(4 * n + 2 * g, 2)
                    keep_lo(T_M + 2 * n + g, m_lo[:, sl, :], bank[4 + g][:].rearrange("p (k t) -> p k t", k=2),
                            m_hi[:, sl, :])

            def mix_pair(n, first):
                c8 = 8 * C_MIX + n * 16
                for u in range(UNITS):
                    if first:
                        attention(8 * C_MIX + u)
                        if u == 3:
                            dve.wait_ge(stats, 12)
                            link(dve.reciprocal(rstdy, rstdy))
                            for b in range(BLOCKS):
                                v = y[:, b, 0:HA * P].rearrange("p (h d) -> p h d", h=HA)
                                r = rstdy[:, b * HA:(b + 1) * HA].rearrange("p (h a) -> p h a", a=1)\
                                    .broadcast_to([P, HA, P])
                                dve.tensor_tensor(v, v, r, ALU.mult).then_inc(y_scaled, 1)
                        if u >= 1:
                            keep_y(u - 1)
                    else:
                        if u == 1:
                            mix_a(n - 1)
                        if u == 4:
                            keep_mix(n - 1)
                    split_ahead(c8, u)
                for u in range(UNITS):
                    if first and u == 0:
                        keep_y(7)
                    if u == 5:
                        mix_b(n)
                    split_ahead(c8 + 8, u)

            mix_pair(0, True)
            with dve.Fori(1, N_MIX) as n:
                mix_pair(n, False)

            def keep_out(j):
                ps = [bank[2 * ((C_OUT + j) % 2) + b] for b in range(BLOCKS)]
                cols = slice(j * CW, (j + 1) * CW)
                for b in range(BLOCKS):
                    dve.wait_ge(o_squared, 2 * j + b + 1)
                    dve.tensor_tensor(og[:, b, cols], ps[b][:], g_post[:, cols], ALU.mult).then_inc(acc_free, 1)

            for j in range(4):
                for u in range(UNITS):
                    if j == 0 and u == 1:
                        mix_a(N_MIX - 1)
                        dve.wait_ge(tail_landed, 48)
                    if j == 0 and u == 4:
                        keep_mix(N_MIX - 1)
                    if j >= 1 and u == 1:
                        keep_out(j - 1)
                    split_ahead(8 * (C_OUT + j), u)
            keep_out(3)
            dve.tensor_reduce(ss1t, ss1.rearrange("p (b j) -> p b j", b=BLOCKS), AX.X, ALU.add).then_inc(norm, 1)
            dve.wait_ge(acc_free, 2 * C_FF)
            dve.wait_ge(stats, 13)
            link(dve.reciprocal(rstd1, rstd1))

            def new_stream(j):
                cols = slice(j * CW, (j + 1) * CW)
                dst = (rows, gate_b)[j % 2]
                for b in range(BLOCKS):
                    dve.scalar_tensor_tensor(h2[:, b, cols], og[:, b, cols], rstd1[:, b:b + 1], h2[:, b, cols],
                                             ALU.mult, ALU.add).then_inc(hg_part, 1)
                if j >= 2:
                    dve.wait_ge(turned, T_H + 2 * (j - 1))
                for b in range(BLOCKS):
                    dve.wait_ge(hg_part, 2 * j + b + 1)
                    dve.tensor_tensor(dst[:, b, :], h2[:, b, cols], g_ffpre[:, cols], ALU.mult)\
                       .then_inc(hg_ready, 1)

            def keep_stream(j):
                for g in range(2):
                    sl = slice(4 * j + 2 * g, 4 * j + 2 * g + 2)
                    keep_lo(T_H + 2 * j + g, f_lo[:, sl, :],
                            bank[4 + 2 * (j % 2) + g][:].rearrange("p (k t) -> p k t", k=2), f_hi[:, sl, :])

            for j in range(4):
                new_stream(j)
                if j:
                    keep_stream(j - 1)
            keep_stream(3)
            dve.wait_ge(stats, 13 + 8)
            dve.tensor_reduce(ss2t, ss2[:].rearrange("p (b j) -> p b j", b=BLOCKS), AX.X, ALU.add)\
               .then_inc(norm, 1)
            dve.wait_ge(stats, 14 + 8)
            dve.reciprocal(rstd2, rstd2).then_inc(norm, 1)

            def square_rows(q, j):
                for b in range(BLOCKS):
                    dve.wait_ge(acc_free, 2 * (C_FF + j) + b + 1 + q * 16)
                    dve.tensor_tensor(rows[:, b, :], rows[:, b, :], rows[:, b, :], ALU.mult)\
                       .then_inc(act_ready, 1)

            def keep_hidden(q, j):
                for g in range(2):
                    sl = slice(4 * j + 2 * g, 4 * j + 2 * g + 2)
                    keep_lo(T_F + 2 * j + g + q * 8, hid_lo[:, sl, :],
                            bank[4 + 2 * (j % 2) + g][:].rearrange("p (k t) -> p k t", k=2), hid_hi[:, sl, :])

            def add_ff2(q, j):
                ps = [bank[2 * ((C_FF + 4 + j) % 2) + b] for b in range(BLOCKS)]
                cols = slice(j * CW, (j + 1) * CW)
                dve.wait_ge(facc_zero, 1)
                dve.wait_ge(used, 8 * (C_FF + 4 + j + 1) + q * 64)
                for b in range(BLOCKS):
                    dve.tensor_tensor(facc[:, b, cols], facc[:, b, cols], ps[b][:], ALU.add).then_inc(acc_free, 1)

            def quarter(q, last):
                for j in range(8):
                    for u in range(UNITS):
                        if 1 <= j <= 4:
                            if u == 1:
                                square_rows(q, j - 1)
                            if u == 4:
                                keep_hidden(q, j - 1)
                        if j >= 5 and u == 1:
                            add_ff2(q, j - 5)
                        if not (last and j == 7 and u + LEAD >= UNITS):
                            split_lo((u + LEAD) % UNITS, 8 * (C_FF + j) + u + LEAD + 1 + q * 64)
                add_ff2(q, 3)

            with dve.Fori(0, QUARTERS - 1) as q:
                quarter(q, False)
            quarter(QUARTERS - 1, True)
            dve.wait_ge(g2_landed, 16)
            dve.wait_ge(f_squared, 8)
            dve.tensor_reduce(ss3t, ss3[:].rearrange("p (b j) -> p b j", b=BLOCKS), AX.X, ALU.add)\
               .then_inc(norm, 1)
            for b in range(BLOCKS):
                link(dve.tensor_tensor(facc[:, b, :], facc[:, b, :], g_ffpost[:], ALU.mult))
            dve.wait_ge(stats, 15 + 8)
            link(dve.reciprocal(rstd3, rstd3))
            for b in range(BLOCKS):
                dve.scalar_tensor_tensor(facc[:, b, :], facc[:, b, :], rstd3[:, b:b + 1], h2[:, b, :],
                                         ALU.mult, ALU.add).then_inc(out_ready, 1)

        @block.tensor
        def _(pe):
            def turn4(dst, pieces):
                for i, v in enumerate(pieces):
                    ins = pe.transpose(dst[:, i * P:(i + 1) * P], v, ident[:])
                return ins

            def multiply(c8, u, hi_of, lo_of, ps, width=CW, first=0, last=UNITS - 1, meta=None):
                pe.wait_ge(lo_ready, c8 + u + 1)
                for k in range(UK):
                    kt = (u - first) * UK + k
                    a, z = u == first and k == 0, u == last and k == UK - 1
                    wh, wl = w_hi[:, u, k, 0:width], w_lo[:, u, k, 0:width]
                    for b in range(BLOCKS):
                        pe.matmul(ps[b][:, 0:width], hi_of(kt, b), wh, start=a, stop=False)
                        pe.matmul(ps[b][:, 0:width], hi_of(kt, b), wl, start=False, stop=False)
                        ins = pe.matmul(ps[b][:, 0:width], lo_of(kt, b), wh, start=False, stop=z)
                if meta is not None:
                    if u == 0 and meta > 0:
                        pe.wait_ge(meta_ready, meta)
                    for k in range(UK):
                        kt = u * UK + k
                        a, z = kt == 0, kt == KT - 1
                        pe.matmul(MB[:, 0:width], u_hi[:, kt, 0:P], w_hi[:, u, k, 0:width], start=a, stop=False)
                        ins = pe.matmul(MB[:, 0:width], u_hi[:, kt, 0:P], w_lo[:, u, k, 0:width], start=False,
                                        stop=z)
                ins.then_inc(used, 1)

            def rows_of(t_hi, t_lo, off=0):
                return (lambda kt, b: t_hi[:, kt, off + b * P:off + (b + 1) * P],
                        lambda kt, b: t_lo[:, kt, b * P:(b + 1) * P])

            pe.wait_ge(consts_landed, 32)
            for i in range(8):
                pe.wait_ge(xg_ready, i + 1)
                turn4(bank[i], [xg[:, i, k * P:(k + 1) * P] for k in range(4)]).then_inc(turned, 1)
            pe.wait_ge(xg_ready, 9)
            pe.wait_ge(turned_lo, 1)
            for kt in range(KT):
                ins = pe.transpose(bank[0][:, kt * 32:(kt + 1) * 32], xm[:, kt * P:(kt + 1) * P],
                                   ident[0:32, 0:32])
            ins.then_inc(turned, 1)
            pe.wait_ge(rel_landed, 16)
            pe.wait_ge(turned_lo, 3)
            for w in range(2):
                ins = pe.matmul(bank[1 + w][0:HA + HB, 0:TAB], relx[:], buck[:, w, :], start=True, stop=True)
            ins.then_inc(table_ready, 1)

            def turn_rows(kind, i):
                n = TURN_NO[(kind, i)]
                if n:
                    pe.wait_ge(proj_kept, n)
                if kind == "kvb":
                    pe.wait_ge(acc_free, 2)
                    pe.wait_ge(meta_ready, 1)
                    pe.wait_ge(small_landed, 7 * 16)
                    for g in range(HKV):
                        for b in range(BLOCKS):
                            pe.transpose(S0[:, (2 * g + b) * P:(2 * g + b + 1) * P],
                                         rows[:, b, g * P:(g + 1) * P], ident[:])
                    for g in range(HKV):
                        pe.matmul(S1[:, g * META:(g + 1) * META], rows_m[:, g * P:(g + 1) * P], fold_m[:],
                                  start=True, stop=True)
                    pe.matmul(S1[0:META, 64:64 + P], fold_m[:], rows_m[:, 2 * P:3 * P], start=True, stop=True)\
                      .then_inc(proj_turned, 1)
                    return
                if kind == "va":
                    pe.wait_ge(meta_ready, {0: 3, 1: 5}[i])
                    pe.matmul(TB[0:META, :], fold_m[:], rows_m[:], start=True, stop=True).then_inc(proj_turned, 1)
                    return
                c = {"qb": C_QB + i, "qa": C_A + 3 * i, "ka": C_A + 3 * i + 1}[kind]
                pe.wait_ge(acc_free, 2 * (c + 1))
                if kind == "ka":
                    pe.wait_ge(meta_ready, {0: 2, 1: 4}[i])
                    pe.wait_ge(o_kept, {0: 4, 1: 8}[i])
                    for g in range(4):
                        pe.matmul(S1[:, g * META:(g + 1) * META], rows_m[:, g * P:(g + 1) * P], fold_m[:],
                                  start=True, stop=True)
                for g, dst in enumerate((S0, TB)):
                    ins = turn4(dst, [rows[:, b, (2 * g + k) * P:(2 * g + k + 1) * P]
                                      for k in range(2) for b in range(BLOCKS)])
                ins.then_inc(proj_turned, 1)

            def kept_by(tau):
                return sum(1 for at in TURN_AT if at < tau)

            def job_scores(j):
                windowed = j < HB // 2
                s0 = 1 if windowed else 0
                n0 = P + META + s0
                pe.wait_ge(proj_kept, kept_by(START[j]))
                if windowed:
                    pe.wait_ge(kb_zero, 1)
                    if j:
                        pe.wait_ge(o_kept, j)
                elif j == HB // 2:
                    pe.wait_ge(o_kept, j)
                for e, S in enumerate((S0, S1)):
                    rows_ = slice(64 * e, 64 * e + 64)
                    q, k = (qbT[rows_, j, :], kbT[rows_, j // 4, :]) if windowed else \
                           (qaT[rows_, j - 8, :], kaT[rows_, j - 8, :])
                    pe.matmul(S[:, 0:n0], q[:, 0:P], k[:, 0:n0], start=True, stop=True)
                    ins = pe.matmul(S[:, n0:2 * n0 + P], q[:, P:2 * P], k[:, 0:n0 + P], start=True, stop=True)
                ins.then_inc(scores_ready, 1)

            def job_turn(j):
                windowed = j < HB // 2
                s0 = 1 if windowed else 0
                n0 = P + META + s0
                pe.wait_ge(probs_ready, j + 1)
                pe.wait_ge(proj_kept, kept_by(START[j] + 3))
                if j > HB // 2:
                    pe.wait_ge(o_kept, j)
                if j == HB // 2:
                    pe.wait_ge(meta_ready, 5)
                for e, dst in enumerate((TB, S0) if windowed else (TB,)):
                    r0 = s0 + META
                    pe.transpose(dst[:, 0:P], t[:, e, r0:r0 + P], ident[:])
                    pe.transpose(dst[:, P:2 * P], t[:, e, n0 + r0:n0 + r0 + P], ident[:])
                    pe.transpose(dst[:, 2 * P:3 * P], t[:, e, n0 + r0 + P:n0 + r0 + 2 * P], ident[:])
                    pe.transpose(dst[0:META, 3 * P:4 * P], t[:, e, s0:r0], ident[:])
                    m1 = S1[0:META, e * P:(e + 1) * P] if windowed else MB[0:META, 0:P]
                    ins = pe.transpose(m1, t[:, e, n0 + s0:n0 + r0], ident[:])
                ins.then_inc(probs_turned, 1)

            def job_values(j):
                windowed = j < HB // 2
                pe.wait_ge(pT_kept, j + 1)
                pe.wait_ge(pTm_kept, j + 1)
                for e in range(2 if windowed else 1):
                    if windowed:
                        col, dv, g = slice((j // 4) * DHB, (j // 4 + 1) * DHB), DHB, None
                        vm, vr = vb_m[:, col], [vb[:, b, col] for b in range(BLOCKS)]
                    else:
                        h = j - HB // 2
                        col = slice(h * P, (h + 1) * P)
                        vm, vr = va_m[:, col], [va[:, b, col] for b in range(BLOCKS)]
                    for q in range(2):
                        o = S1[:, 2 * P + q * P + e * DHB:2 * P + q * P + (e + 1) * DHB] if windowed else \
                            MB[:, P + q * P:P + (q + 1) * P]
                        pe.matmul(o, pTm[:, e, q * P:(q + 1) * P], vm, start=True, stop=False)
                        ins = pe.matmul(o, pT[:, e, q * P:(q + 1) * P], vr[0], start=False, stop=q == 0)
                        if q == 1:
                            ins = pe.matmul(o, pT[:, e, 2 * P:3 * P], vr[1], start=False, stop=True)
                ins.then_inc(o_ready, 1)

            def attention(tau):
                for j in range(JOBS):
                    if tau == START[j] + 4:
                        job_values(j)
                for j in range(JOBS):
                    if tau == START[j] + 3:
                        job_turn(j)
                if tau in TURN_AT:
                    turn_rows(*TURN_AT[tau])
                for j in range(JOBS):
                    if tau == START[j]:
                        job_scores(j)

            x_hi, x_lo = rows_of(u_hi, u_lo, 2 * META)
            pe.wait_ge(turned_lo, 9)
            pe.wait_ge(table_copied, 1)
            for c in range(C_MIX):
                ps = [bank[2 * (c % 2) + b] for b in range(BLOCKS)]
                if c >= 2:
                    pe.wait_ge(acc_free, 2 * (c - 1))
                for u in range(UNITS):
                    multiply(8 * c, u, x_hi, x_lo, ps, 256 if c == 0 else CW,
                             meta=META_WAIT.get(c))
                    attention(8 * c + u)

            def turn_y(i):
                g = (i + 4) % 8
                if i >= 2:
                    pe.wait_ge(turned_lo, T_Y + i - 1)
                if i == 4:
                    pe.wait_ge(y_scaled, 2)
                turn4(bank[4 + i % 2], [y[:, b, (2 * g + k) * P:(2 * g + k + 1) * P]
                                        for k in range(2) for b in range(BLOCKS)]).then_inc(turned, 1)

            def turn_mix(n):
                pe.wait_ge(mix_ready, 2 + n * 2)
                pe.wait_ge(turned_lo, T_M + n * 2)
                for g in range(2):
                    turn4(bank[4 + g], [rows[:, b, (2 * g + k) * P:(2 * g + k + 1) * P]
                                        for k in range(2) for b in range(BLOCKS)]).then_inc(turned, 1)

            yb_hi, yb_lo = rows_of(y_hi, y_lo)

            def mix_pair(n, first):
                c8 = 8 * C_MIX + n * 16
                pe.wait_ge(acc_free, 2 * (C_MIX - 1) + n * 4)
                for u in range(UNITS):
                    multiply(c8, u, x_hi, x_lo, [bank[2], bank[3]])
                    if first:
                        attention(8 * C_MIX + u)
                        turn_y(u)
                    elif u == 3:
                        turn_mix(n - 1)
                pe.wait_ge(acc_free, 2 * C_MIX + n * 4)
                for u in range(4):
                    if first and u == 0:
                        pe.wait_ge(turned_lo, T_Y + 4)
                    multiply(c8 + 8, u, lambda kt, b: yb_hi(kt + 8, b), lambda kt, b: yb_lo(kt + 8, b),
                             [bank[0], bank[1]], last=3)
                if first:
                    pe.wait_ge(turned_lo, T_Y + 8)
                else:
                    pe.wait_ge(mix_ready, n * 2)
                for u in range(4, UNITS):
                    multiply(c8 + 8, u, yb_hi, yb_lo, [bank[6], bank[7]], first=4)

            mix_pair(0, True)
            with pe.Fori(1, N_MIX) as n:
                mix_pair(n, False)

            m = rows_of(m_hi, m_lo)
            for j in range(4):
                c = C_OUT + j
                pe.wait_ge(acc_free, 2 * (c - 1))
                for u in range(UNITS):
                    if j == 0 and u == 6:
                        pe.wait_ge(turned_lo, T_H)
                    multiply(8 * c, u, *m, [bank[2 * (c % 2) + b] for b in range(BLOCKS)])
                    if j == 0 and u == 3:
                        turn_mix(N_MIX - 1)

            for j in range(4):
                pe.wait_ge(hg_ready, 2 * (j + 1))
                if j >= 2:
                    pe.wait_ge(turned_lo, T_H + 2 * (j - 1))
                src = (rows, gate_b)[j % 2]
                for g in range(2):
                    turn4(bank[4 + 2 * (j % 2) + g], [src[:, b, (2 * g + k) * P:(2 * g + k + 1) * P]
                                                      for k in range(2) for b in range(BLOCKS)])\
                        .then_inc(turned, 1)
            pe.wait_ge(turned_lo, T_F)

            def turn_hidden(q, j):
                pe.wait_ge(act_ready, 2 * (j + 1) + q * 8)
                pe.wait_ge(turned_lo, T_F + 2 * (j - 1) + q * 8)
                for g in range(2):
                    turn4(bank[4 + 2 * (j % 2) + g], [rows[:, b, (2 * g + k) * P:(2 * g + k + 1) * P]
                                                      for k in range(2) for b in range(BLOCKS)])\
                        .then_inc(turned, 1)

            f, hid = rows_of(f_hi, f_lo), rows_of(hid_hi, hid_lo)

            def quarter(q):
                for j in range(8):
                    c = C_FF + j
                    pe.wait_ge(acc_free, 2 * (c - 1) + q * 16)
                    if j == 4:
                        pe.wait_ge(turned_lo, T_F + 6 + q * 8)
                    for u in range(UNITS):
                        if j == 4 and u == 6:
                            pe.wait_ge(turned_lo, T_F + 8 + q * 8)
                        multiply(8 * c + q * 64, u, *(f if j < 4 else hid),
                                 [bank[2 * (c % 2) + b] for b in range(BLOCKS)])
                        if 1 <= j <= 4 and u == 3:
                            turn_hidden(q, j - 1)

            with pe.Fori(0, QUARTERS) as q:
                quarter(q)


def has_meta(c):
    return c == 0 or (C_A <= c < C_GA and (c - C_A) % 3 > 0)


META_WAIT = {0: 0, 4: 1, 5: 2, 7: 3, 8: 4}

_INS = ["x", "meta_tokens", "rel_bias", "w_in", "w_branch_a", "w_branch_b", "w_out", "lambda_q1", "lambda_k1",
        "lambda_q2", "lambda_k2", "diff_norm", "sinks", "norm_attn_pre", "norm_attn_post", "w_ff1", "w_ff2",
        "norm_ff_pre", "norm_ff_post"]


def kernel(**inputs):
    import concourse.bacc as bacc
    from concourse.bass_utils import run_bass_kernel_spmd

    nc = bacc.Bacc("TRN2", target_bir_lowering=False, num_devices=1)
    given = {name: np.ascontiguousarray(inputs[name]) for name in _INS}
    given["identity"] = np.eye(P, dtype=np.float32)
    given["fold"] = np.concatenate([np.eye(META, dtype=np.float32)] * 2)
    given["buckets"] = bucket_table()
    arrays, args = {}, []
    for name, a in given.items():
        arrays[f"in_{name}"] = a
        args.append(nc.dram_tensor(f"in_{name}", a.shape, mybir.dt.from_np(a.dtype), kind="ExternalInput").ap())
    args.append(nc.dram_tensor("out_h", (1, SEQ, D), F32, kind="ExternalOutput").ap())
    hybrid_block(nc, *args)
    r = run_bass_kernel_spmd(nc, [arrays], core_ids=[0])
    return r.results[0]["out_h"]
```

```python
import math
from contextlib import ExitStack

import numpy as np

import concourse.bass as bass
from concourse import mybir

F32 = mybir.dt.float32
F32R = mybir.dt.float32r
ACT = mybir.ActivationFunctionType
ALU = mybir.AluOpType
AX = mybir.AxisListType

P = 128
D = 2048
SEQ = 256
BLOCKS = SEQ // P
META = 16
FF = 4 * D
HA, DHA = 8, 64
HB, HKV, DHB = 16, 2, 64
EPS = 1e-6
NEG = -1e30
LAM_INIT = 0.8 - 0.6 * math.exp(-0.3 * 0)
N_BUCKETS, MAX_DIST, WINDOW = 32, 128, 128

KT = D // P
CW = 512
UNITS = 8
UK = KT // UNITS
LEAD = 5
UT = 2 * META + SEQ

QA0, KA0, VA0 = 0, 1024, 2048
QB0, KB0, VB0 = 3072, 4096, 4224
GA0, GB0 = 4352, 6400

C_QB, C_A, C_GA, C_MIX, C_OUT, C_FF = 1, 3, 9, 13, 21, 25
N_MIX = D // CW
QUARTERS = 4

JOBS = HB // 2 + HA
START = [20 + 6 * j for j in range(HB // 2)] + [72 + 4 * j for j in range(HA)]
TURN_AT = {10: ("kvb", 0), 18: ("qb", 0), 31: ("qb", 1), 37: ("qa", 0), 43: ("ka", 0), 49: ("va", 0),
           61: ("qa", 1), 67: ("ka", 1), 74: ("va", 1)}
START_ORDER = [("x", 0), ("w", 0), ("x", 1), ("w", 1), ("x", 2), ("w", 2), ("x", 3), ("w", 3), ("w", 4),
               ("w", 5), ("w", 6), ("w", 7)]
TURN_NO = {g: n for n, g in enumerate(TURN_AT.values())}

T_Y = 8
T_M = T_Y + 8
T_H = T_M + 2 * N_MIX
T_F = T_H + 8

TAB = 400


def bucket_table():
    dist = np.arange(TAB) - 127
    n = np.maximum(dist, 0)
    exact = N_BUCKETS // 2
    nf = np.maximum(n, 1).astype(np.float32)
    large = exact + (np.log(nf / np.float32(exact)) / np.float32(math.log(MAX_DIST / exact))
                     * np.float32(N_BUCKETS - exact)).astype(np.int32)
    b = np.where(n < exact, n, np.minimum(large, N_BUCKETS - 1))
    out = np.zeros((N_BUCKETS + 1, 2, TAB), np.float32)
    for w, ok in enumerate((dist >= 0, (dist >= 0) & (dist < WINDOW))):
        out[b[ok], w, np.arange(TAB)[ok]] = 1.0
        out[N_BUCKETS, w, ~ok] = NEG
    return out


def hybrid_block(nc, x, meta_tokens, rel_bias, w_in, w_branch_a, w_branch_b, w_out, lambda_q1, lambda_k1,
                 lambda_q2, lambda_k2, diff_norm, sinks, norm_attn_pre, norm_attn_post, w_ff1, w_ff2,
                 norm_ff_pre, norm_ff_post, identity, fold, buckets, out):
    table = nc.dram_tensor("bias_table", (2, HA + HB, TAB), F32)

    ctx = ExitStack()
    with ctx:
        def sb(name, shape, dt=F32):
            return ctx.enter_context(nc.sbuf_tensor(name, shape, dt))

        def sem(name):
            return ctx.enter_context(nc.semaphore(name))

        def region(kb4, *groups):
            made = []
            for group in groups:
                with ExitStack() as g:
                    made.append([g.enter_context(nc.sbuf_tensor(*t)) for t in group])
            sb(f"keep_{groups[0][0][0]}", [P, kb4])
            return made

        (raw,), (w_lo,) = region(UNITS * UK * CW, [("raw", [P, UNITS, UK, CW], F32)],
                                 [("w_lo", [P, UNITS, UK, CW], F32R)])
        w_hi = sb("w_hi", [P, UNITS, UK, CW], F32R)

        (u_hi, u_lo), (h2, g_post, g_ffpre), (g_ffpost_keep, g_ffpost) = region(
            KT * (UT + SEQ),
            [("u_hi", [P, KT, UT], F32R), ("u_lo", [P, KT, SEQ], F32R)],
            [("h2", [P, BLOCKS, D], F32), ("g_post", [P, D], F32), ("g_ffpre", [P, D], F32)],
            [("g_ffpost_keep", [P, BLOCKS, D], F32), ("g_ffpost", [P, D], F32)])

        (qbT, kbT, vb, vb_m, qaT, kaT, va, va_m), (y_hi, y_lo), (f_hl,) = region(
            10400,
            [("qbT", [P, HB // 2, SEQ], F32), ("kbT", [P, HKV, 1 + META + SEQ], F32),
             ("vb", [P, BLOCKS, HKV * DHB], F32), ("vb_m", [META, HKV * DHB], F32),
             ("qaT", [P, HA, SEQ], F32), ("kaT", [P, HA, META + SEQ], F32),
             ("va", [P, BLOCKS, HA * P], F32), ("va_m", [META, HA * P], F32)],
            [("y_hi", [P, KT, SEQ], F32R), ("y_lo", [P, KT, SEQ], F32R)],
            [("f_hl", [P, KT, 2 * SEQ], F32R)])

        (y, t, pT, pTm, bias), (m_hi, m_lo), (hid_hi, hid_lo), (xs,) = region(
            2 * KT * SEQ,
            [("y", [P, BLOCKS, 2 * HA * P], F32), ("t", [P, 2, 418], F32), ("pT", [P, 2, 3 * P], F32),
             ("pTm", [META, 2, 2 * P], F32), ("bias", [P, 2, 2, 418], F32)],
            [("m_hi", [P, KT, SEQ], F32R), ("m_lo", [P, KT, SEQ], F32R)],
            [("hid_hi", [P, KT, SEQ], F32R), ("hid_lo", [P, KT, SEQ], F32R)],
            [("xs", [P, BLOCKS, D], F32)])

        (ga,), (og,), (facc,), (xm, g_rows, g_col, meta_g) = region(
            BLOCKS * D, [("ga", [P, BLOCKS, D], F32)], [("og", [P, BLOCKS, D], F32)],
            [("facc", [P, BLOCKS, D], F32)],
            [("xm", [2 * META, D], F32), ("g_rows", [KT, P], F32), ("g_col", [P, KT], F32),
             ("meta_g", [P, KT, META], F32)])

        rows = sb("rows", [P, BLOCKS, CW])
        hid_rows = rows[:].rearrange("p b (g t) -> p (b g) t", t=SEQ)
        rows_m = sb("rows_m", [2 * META, CW])
        gate_b = sb("gate_b", [P, BLOCKS, CW])
        ident = sb("ident", [P, P])
        fold_m = sb("fold_m", [2 * META, META])
        relx = sb("relx", [N_BUCKETS + 1, HA + HB])
        buck = sb("buck", [N_BUCKETS + 1, 2, TAB])
        lam_v = sb("lam_v", [P, 4, DHA])
        dcol = sb("dcol", [P, 1])
        sink_bc = sb("sink_bc", [P, HB])
        sc = sb("sc", [P, 96])
        eps = sc[:, 0:1]
        ssx, rstd, rstd8 = sc[:, 2:4], sc[:, 4:6], sc[:, 6:8]
        ssm, rstdm = sc[0:32, 8:9], sc[0:32, 9:10]
        lam_dot, lam_exp, neg_lam = sc[:, 10:12], sc[:, 12:14], sc[:, 14:15]
        mx, nmx, sums, rs, cc = sc[:, 16:20], sc[:, 20:24], sc[:, 24:28], sc[:, 28:32], sc[:, 32:34]
        ssy, rstdy = sc[:, 36:52], sc[:, 52:68]
        ss1, ss1t, rstd1 = sc[:, 68:76], sc[:, 76:78], sc[:, 78:80]
        ss2t, rstd2 = sc[:, 80:82], sc[:, 82:84]
        ss3t, rstd3 = sc[:, 84:86], sc[:, 86:88]
        ss2 = sb("ss2", [P, 8])
        ss3 = sb("ss3", [P, 8])

        bank = [ctx.enter_context(nc.psum_tensor(f"bank{i}", [P, 512], F32)) for i in range(8)]
        S0, S1, TB, MB = bank[4:8]

        x_landed = [sem(f"x_landed{i}") for i in range(4)]
        xm_landed, xm_twice, consts_landed = sem("xm_landed"), sem("xm_twice"), sem("consts_landed")
        rel_ones, rel_landed, small_landed = sem("rel_ones"), sem("rel_landed"), sem("small_landed")
        landed = [sem(f"landed{u}") for u in range(UNITS)]
        slot_free = sem("slot_free")
        hi_ready, lo_ready = sem("hi_ready"), sem("lo_ready")
        used = sem("used")
        acc_free = sem("acc_free")
        eps_set = sem("eps_set")
        gain_turned, gain_ready = sem("gain_turned"), sem("gain_ready")
        meta_turned, meta_scaled = sem("meta_turned"), sem("meta_scaled")
        meta_hi_ready, meta_lo_ready = sem("meta_hi_ready"), sem("meta_lo_ready")
        turned, turned_hi, turned_lo = sem("turned"), sem("turned_hi"), sem("turned_lo")
        stats = sem("stats")
        norm = sem("norm")
        dve_seq = sem("dve_seq")
        table_ready, table_copied, table_stored = sem("table_ready"), sem("table_copied"), sem("table_stored")
        bias_landed = [sem(f"bias_landed{i}") for i in range(2)]
        sink_set, kb_zero = sem("sink_set"), sem("kb_zero")
        meta_ready = sem("meta_ready")
        proj_turned, proj_kept = sem("proj_turned"), sem("proj_kept")
        scores_ready, max_ready, exp_done, probs_ready = (sem("scores_ready"), sem("max_ready"),
                                                          sem("exp_done"), sem("probs_ready"))
        probs_turned, pT_kept, pTm_kept = sem("probs_turned"), sem("pT_kept"), sem("pTm_kept")
        o_ready, o_kept, ssy_ready = sem("o_ready"), sem("o_kept"), sem("ssy_ready")
        y_scaled = sem("y_scaled")
        gates_ready = sem("gates_ready")
        mix_part, mix_ready = sem("mix_part"), sem("mix_ready")
        g_post_landed, tail_landed = sem("g_post_landed"), sem("tail_landed")
        o_squared, hg_part, hg_ready = sem("o_squared"), sem("hg_part"), sem("hg_ready")
        facc_zero = sem("facc_zero")
        hid_copied, hid_summed, hid_ready = sem("hid_copied"), sem("hid_summed"), sem("hid_ready")
        hid_hi_ready, hid_lo_ready = sem("hid_hi_ready"), sem("hid_lo_ready")
        g2_landed, f_squared, f_gained = sem("g2_landed"), sem("f_squared"), sem("f_gained")
        last_rows = sem("last_rows")
        out_ready, stored = sem("out_ready"), sem("stored")

        xf = x[0].rearrange("(b p) d -> p b d", p=P)
        outf = out[0].rearrange("(b p) d -> p b d", p=P)

        def unit_of(w, krange, nrange):
            return w[0, krange, nrange].rearrange("(k p) n -> p k n", p=P)

        def w_in_column(c):
            if c == 0:
                return KB0
            if c < C_A:
                return QB0 + (c - C_QB) * CW
            if c < C_GA:
                i, kind = divmod(c - C_A, 3)
                return (QA0, KA0, VA0)[kind] + i * CW
            return GA0 + (c - C_GA) * CW

        def bcast(v, n=P):
            return v.partition_broadcast(n)

        block = ctx.enter_context(nc.Block())

        @block.sync
        def _(sp):
            def load(u, w, krange, nrange, free, width=CW):
                if free is not None:
                    sp.wait_ge(used, free)
                    sp.sem_inc(slot_free, 1)
                sp.dma_start(raw[:, u, :, 0:width], unit_of(w, krange, nrange)).then_inc(landed[u], 16)

            sp.dma_start(ident[:], identity).then_inc(consts_landed, 16)
            sp.dma_start(g_rows[:], norm_attn_pre[0].rearrange("(k p) -> k p", p=P)).then_inc(consts_landed, 16)
            for step, i in START_ORDER:
                if step == "x":
                    cols = slice(i * CW, (i + 1) * CW)
                    sp.dma_start(xs[:, :, cols], xf[:, :, cols]).then_inc(x_landed[i], 16)
                else:
                    load(i, w_in, slice(i * 256, i * 256 + 256), slice(KB0, KB0 + 256), None, 256)
            for c in range(1, C_MIX):
                n0 = w_in_column(c)
                for u in range(UNITS):
                    load(u, w_in, slice(u * 256, u * 256 + 256), slice(n0, n0 + CW), 8 * c + u - 7)
            with sp.Fori(0, N_MIX) as n:
                for u in range(UNITS):
                    load(u, w_in, slice(u * 256, u * 256 + 256), bass.ds(GB0 + n * CW, CW),
                         8 * C_MIX + u - 7 + n * 16)
                for u in range(UNITS):
                    w = w_branch_b if u < 4 else w_branch_a
                    k0 = (u % 4) * 256
                    load(u, w, slice(k0, k0 + 256), bass.ds(n * CW, CW), 8 * C_MIX + 8 + u - 7 + n * 16)
            with sp.Fori(0, N_MIX) as n:
                for u in range(UNITS):
                    load(u, w_out, slice(u * 256, u * 256 + 256), bass.ds(n * CW, CW),
                         8 * C_OUT + u - 7 + n * 8)
            with sp.Fori(0, QUARTERS) as q:
                for j in range(4):
                    for u in range(UNITS):
                        load(u, w_ff1, slice(u * 256, u * 256 + 256), bass.ds(q * D + j * CW, CW),
                             8 * (C_FF + j) + u - 7 + q * 64)
                for j in range(4):
                    for u in range(UNITS):
                        load(u, w_ff2, bass.ds(q * D + u * 256, 256), slice(j * CW, j * CW + CW),
                             8 * (C_FF + 4 + j) + u - 7 + q * 64)
            for b in range(BLOCKS):
                for j in range(4):
                    cols = slice(j * CW, (j + 1) * CW)
                    sp.wait_ge(out_ready, 4 * b + j + 1)
                    sp.dma_start(outf[:, b, cols], facc[:, b, cols]).then_inc(stored, 16)
            sp.wait_ge(stored, 16 * 4 * BLOCKS)

        @block.gpsimd
        def _(pool):
            pool.memset(relx[:], 1.0).then_inc(rel_ones, 1)
            pool.memset(kbT[:, :, 0:1], 0.0).then_inc(kb_zero, 1)
            for i, v in enumerate((lambda_q1, lambda_k1, lambda_q2, lambda_k2)):
                pool.dma_start(lam_v[:, i, :], bcast(v[0])).then_inc(small_landed, 16)
            pool.dma_start(dcol[:], diff_norm[0].rearrange("(p a) -> p a", a=1)).then_inc(small_landed, 16)
            pool.dma_start(sink_bc[:], bcast(sinks[0])).then_inc(small_landed, 16)
            pool.dma_start(fold_m[:], fold).then_inc(small_landed, 16)

            def job_bias(j):
                slot = j % 2
                if j >= 2:
                    pool.wait_ge(max_ready, j - 1)
                if j < HB // 2:
                    row = HA + 2 * j
                    for w, t0, at, n in ((1, 0, 0, 128), (0, 128, 128, META), (1, 0, 145, 256),
                                         (0, 256, 401, META)):
                        src = bass.AP(table, (w * (HA + HB) + row) * TAB + t0, [[1, P], [TAB, 2], [1, n]])
                        pool.dma_start(bias[:, slot, :, at:at + n], src).then_inc(bias_landed[slot], 16)
                    v = bias[:, slot, :, :]
                    for e in range(2):
                        for at in (144, 417):
                            last = pool.tensor_copy(v[:, e, at:at + 1], sink_bc[:, 2 * j + e:2 * j + e + 1])
                    last.then_inc(sink_set, 1)
                else:
                    src = bass.AP(table, (j - HB // 2) * TAB, [[1, P], [1, META + SEQ]])
                    pool.dma_start(bias[:, slot, 0, 0:META + SEQ], src).then_inc(bias_landed[slot], 16)

            pool.wait_ge(small_landed, 7 * 16)
            pool.wait_ge(table_copied, 1)
            pool.dma_start(table.ap().rearrange("w h t -> h w t"), rows[0:HA + HB, :, 0:TAB])\
                .then_inc(table_stored, 16)
            pool.wait_ge(table_stored, 16)
            for j in range(JOBS):
                job_bias(j)
            pool.wait_ge(norm, 5)
            pool.memset(facc[:], 0.0).then_inc(facc_zero, 1)

        @block.scalar
        def _(act):
            def split_hi(u, chunk, width=CW):
                act.wait_ge(landed[u], 16 + 16 * chunk)
                act.activation(w_hi[:, u, :, 0:width], raw[:, u, :, 0:width], ACT.Copy).then_inc(hi_ready, 1)

            def split_ahead(c, u):
                uu = (u + LEAD) % UNITS
                split_hi(uu, c + (u + LEAD) // UNITS)

            def keep_hi(n, dst, src, scale=None):
                act.wait_ge(turned, n + 1)
                if scale is None:
                    act.activation(dst, src, ACT.Copy).then_inc(turned_hi, 1)
                else:
                    act.activation(dst, src, ACT.Identity, scale=scale).then_inc(turned_hi, 1)

            act.dma_start(xm[0:META, :], meta_tokens).then_inc(xm_landed, 16)
            act.wait_ge(eps_set, 1)
            act.activation(sc[:, 1:2], eps, ACT.Copy)
            act.wait_ge(rel_ones, 1)
            act.dma_start(relx[0:N_BUCKETS, :], rel_bias).then_inc(rel_landed, 16)
            act.dma_start(buck[:], buckets).then_inc(rel_landed, 16)
            act.dma_start(xm[META:2 * META, :], meta_tokens).then_inc(xm_twice, 16)

            def keep_x(i):
                act.wait_ge(turned, i + 1)
                for k in range(2):
                    kt = 2 * i + k
                    last = act.activation(u_hi[:, kt, 2 * META:], bank[2 + i % 4][:, k * SEQ:(k + 1) * SEQ],
                                          ACT.Identity, scale=g_col[:, kt:kt + 1])
                last.then_inc(turned_hi, 1)

            act.wait_ge(gain_ready, 1)
            for step, i in START_ORDER:
                if step == "x":
                    keep_x(2 * i)
                    keep_x(2 * i + 1)
                else:
                    split_hi(i, 0, 256)
                if (step, i) == ("w", 0):
                    act.wait_ge(meta_scaled, 1)
                    act.activation(u_hi[:, :, 0:META], meta_g[:], ACT.Copy).then_inc(meta_hi_ready, 1)

            def square_x(n):
                b, j = divmod(n, 4)
                if n:
                    act.wait_ge(stats, n)
                act.activation(gate_b[:, 0, :], xs[:, b, j * CW:(j + 1) * CW], ACT.Square,
                               accum_out=ss3[:, n:n + 1]).then_inc(stats, 1)

            for u in range(UNITS - LEAD, UNITS):
                if u < UNITS - 1:
                    square_x(2 * (u - UNITS + LEAD))
                    square_x(2 * (u - UNITS + LEAD) + 1)
                split_ahead(0, u)
            act.wait_ge(norm, 1)
            act.activation(rstd, ssx, ACT.Sqrt, scale=1.0 / D, bias=eps).then_inc(stats, 1)
            act.activation(rstdm, ssm, ACT.Sqrt, scale=1.0 / D, bias=eps[0:32, :]).then_inc(stats, 1)
            act.wait_ge(norm, 2)
            act.activation(lam_exp, lam_dot, ACT.Exp).then_inc(stats, 1)

            def keep_meta(c):
                act.wait_ge(used, 8 * (c + 1))
                if c == 0:
                    act.wait_ge(norm, 3)
                    dup = MB[0:32, 0:P].rearrange("p (g a d) -> p g a d", g=HKV, a=1)\
                        .broadcast_to([32, HKV, 2, DHB])
                    act.activation(rows_m[:, 0:2 * P].rearrange("p (g a d) -> p g a d", g=HKV, a=2), dup,
                                   ACT.Identity, scale=rstdm)
                    act.activation(rows_m[:, 2 * P:3 * P], MB[0:32, P:2 * P], ACT.Identity, scale=rstdm)\
                       .then_inc(meta_ready, 1)
                    return
                act.wait_ge(proj_turned, meta_done[c])
                act.activation(rows_m[:], MB[0:32, :], ACT.Identity, scale=rstdm).then_inc(meta_ready, 1)

            meta_done = {4: 1, 5: TURN_NO[("ka", 0)] + 1, 7: TURN_NO[("va", 0)] + 1, 8: TURN_NO[("ka", 1)] + 1}

            def keep_chunk(c):
                ps = [bank[2 * (c % 2) + b] for b in range(BLOCKS)]
                act.wait_ge(used, 8 * (c + 1))
                if c == 0:
                    act.wait_ge(table_stored, 16)
                    for b in range(BLOCKS):
                        dup = ps[b][:, 0:128].rearrange("p (g a d) -> p g a d", g=HKV, a=1)\
                            .broadcast_to([P, HKV, 2, DHB])
                        act.activation(rows[:, b, 0:256].rearrange("p (g a d) -> p g a d", g=HKV, a=2), dup,
                                       ACT.Identity, scale=rstd[:, b:b + 1])
                        act.activation(vb[:, b, :], ps[b][:, 128:256], ACT.Identity,
                                       scale=rstd[:, b:b + 1]).then_inc(acc_free, 1)
                elif c < C_A or (c < C_GA and (c - C_A) % 3 < 2):
                    is_q = c < C_A or (c - C_A) % 3 == 0
                    act.wait_ge(proj_turned, rows_done[c])
                    for b in range(BLOCKS):
                        act.activation(rows[:, b, :], ps[b][:], ACT.Identity,
                                       scale=(rstd8 if is_q else rstd)[:, b:b + 1]).then_inc(acc_free, 1)
                elif c < C_GA:
                    i = (c - C_A) // 3
                    for b in range(BLOCKS):
                        act.activation(va[:, b, i * CW:(i + 1) * CW], ps[b][:], ACT.Identity,
                                       scale=rstd[:, b:b + 1]).then_inc(acc_free, 1)
                else:
                    i = c - C_GA
                    for b in range(BLOCKS):
                        act.activation(ga[:, b, i * CW:(i + 1) * CW], ps[b][:], ACT.Identity,
                                       scale=rstd[:, b:b + 1]).then_inc(acc_free, 1)

            rows_done = {1: 1, 2: 2, 3: 3, 4: 4, 6: 5, 7: 7}

            def job_exp(j):
                s0 = 1 if j < HB // 2 else 0
                n0 = P + META + s0
                act.wait_ge(max_ready, j + 1)
                for e in range(2):
                    for q, (a, b) in enumerate(((0, n0), (n0, 2 * n0 + P))):
                        last = act.activation(t[:, e, a:b], t[:, e, a:b], ACT.Exp,
                                              bias=nmx[:, 2 * e + q:2 * e + q + 1],
                                              accum_out=sums[:, 2 * e + q:2 * e + q + 1])
                last.then_inc(exp_done, 1)

            def job_keep_probs(j):
                act.wait_ge(probs_turned, j + 1)
                for e, src in enumerate((TB, S0) if j < HB // 2 else (TB,)):
                    act.activation(pTm[:, e, 0:P], src[0:META, 3 * P:4 * P], ACT.Copy)
                    last = act.activation(pT[:, e, :], src[:, 0:3 * P], ACT.Copy)
                last.then_inc(pT_kept, 1)

            def job_squares(j):
                h = j - HB // 2
                act.wait_ge(o_kept, j + 1)
                if h:
                    act.wait_ge(ssy_ready, 2 * h)
                for b in range(BLOCKS):
                    act.activation(gate_b[:, b, 0:P], y[:, b, h * P:(h + 1) * P], ACT.Square,
                                   accum_out=ssy[:, b * HA + h:b * HA + h + 1]).then_inc(ssy_ready, 1)

            def attention(tau):
                for j in range(JOBS):
                    if tau == START[j] + 1:
                        job_exp(j)
                    if tau == START[j] + 4:
                        job_keep_probs(j)
                    if tau == START[j] + 6 and j >= HB // 2:
                        job_squares(j)

            for c in range(1, C_MIX):
                for u in range(UNITS):
                    if u == 0 and has_meta(c - 1):
                        keep_meta(c - 1)
                    if u == 1:
                        keep_chunk(c - 1)
                    attention(8 * c + u)
                    split_ahead(c, u)

            def gates(n, sl):
                act.wait_ge(acc_free, 2 * C_MIX)
                for b in range(BLOCKS):
                    act.activation(ga[:, b, sl], ga[:, b, sl], ACT.Sigmoid).then_inc(gates_ready, 1)

            def gate_b_sigmoid(n, c):
                act.wait_ge(used, 8 + 8 * c)
                for b in range(BLOCKS):
                    act.activation(gate_b[:, b, :], bank[2 + b][:], ACT.Sigmoid,
                                   scale=rstd[:, b:b + 1]).then_inc(acc_free, 1)

            def keep_mix(n):
                for g in range(2):
                    keep_hi(T_M + 2 * n + g, m_hi[:, bass.ds(4 * n + 2 * g, 2), :],
                            bank[4 + g][:].rearrange("p (k t) -> p k t", k=2))

            def mix_pair(n, first):
                cg = C_MIX + 2 * n
                for u in range(UNITS):
                    if first:
                        if u == 1:
                            keep_chunk(C_MIX - 1)
                        attention(8 * C_MIX + u)
                        if u == 3:
                            act.wait_ge(ssy_ready, 2 * HA)
                            act.activation(rstdy, ssy, ACT.Sqrt, scale=1.0 / P, bias=eps)\
                               .then_inc(stats, 1)
                        if u >= 1:
                            keep_y(u - 1)
                    elif u == 4:
                        keep_mix(n - 1)
                    if u == 6:
                        gates(n, bass.ds(n * CW, CW))
                    split_ahead(cg, u)
                for u in range(UNITS):
                    if first and u == 0:
                        keep_y(7)
                    if u == 1:
                        gate_b_sigmoid(n, cg)
                    split_ahead(cg + 1, u)

            def keep_y(i):
                g = (i + 4) % 8
                keep_hi(T_Y + i, y_hi[:, 2 * g:2 * g + 2, :],
                        bank[4 + i % 2][:].rearrange("p (k t) -> p k t", k=2), dcol[:] if g < 4 else None)

            mix_pair(0, True)
            with act.Fori(1, N_MIX) as n:
                mix_pair(n, False)

            def square_out(j):
                act.wait_ge(used, 8 * (C_OUT + j + 1))
                ps = [bank[2 * ((C_OUT + j) % 2) + b] for b in range(BLOCKS)]
                if j:
                    act.wait_ge(o_squared, 2 * j)
                for b in range(BLOCKS):
                    act.activation(gate_b[:, b, :], ps[b][:], ACT.Square,
                                   accum_out=ss1[:, b * 4 + j:b * 4 + j + 1]).then_inc(o_squared, 1)

            act.wait_ge(used, 8 * (C_OUT - 1))
            act.dma_start(g_post[:], bcast(norm_attn_post[0])).then_inc(g_post_landed, 16)
            for j in range(4):
                for u in range(UNITS):
                    if u == 2:
                        cols = slice(j * CW, (j + 1) * CW)
                        act.dma_start(h2[:, :, cols], xf[:, :, cols]).then_inc(tail_landed, 16)
                    if j == 1 and u == 6:
                        act.dma_start(g_ffpre[:], bcast(norm_ff_pre[0])).then_inc(tail_landed, 16)
                    if j == 0 and u == 4:
                        keep_mix(N_MIX - 1)
                    if j >= 1 and u == 1:
                        square_out(j - 1)
                    if j == 2 and u == 4:
                        act.activation(ss2t, rstdy[:, 0:2], ACT.Sqrt)
                    split_ahead(C_OUT + j, u)
            square_out(3)
            act.wait_ge(norm, 4)
            act.activation(rstd1, ss1t, ACT.Sqrt, scale=1.0 / D, bias=eps).then_inc(stats, 1)

            def square_h2(j):
                for b in range(BLOCKS):
                    act.activation(og[:, b, j * CW:(j + 1) * CW], h2[:, b, j * CW:(j + 1) * CW], ACT.Square,
                                   accum_out=ss2[:, b * 4 + j:b * 4 + j + 1]).then_inc(stats, 1)

            def keep_stream(j):
                for g in range(2):
                    keep_hi(T_H + 2 * j + g, f_hl[:, 4 * j + 2 * g:4 * j + 2 * g + 2, 0:SEQ],
                            bank[4 + 2 * (j % 2) + g][:].rearrange("p (k t) -> p k t", k=2))

            def copy_hidden(q, j):
                act.wait_ge(used, 8 * (C_FF + j + 1) + q * 64)
                for g in range(4):
                    act.activation(hid_rows[:, g, :], bank[4 * (j % 2) + g][:, 0:SEQ], ACT.Copy)\
                       .then_inc(hid_copied, 1)

            def keep_hidden(q, j):
                act.wait_ge(hid_ready, j + 1 + q * 4)
                act.activation(hid_hi[:, 4 * j:4 * j + 4, :], hid_rows, ACT.Copy).then_inc(hid_hi_ready, 1)

            def quarter(q, first=False, last=False):
                for j in range(8):
                    for u in range(UNITS):
                        if first and j == 0:
                            if u in (1, 3, 5):
                                keep_stream((u + 1) // 2)
                            if u in (0, 2, 4, 6):
                                square_h2(u // 2)
                        if first and j == 1 and u == 0:
                            act.wait_ge(norm, 5)
                            act.activation(rstd2, ss2t, ACT.Sqrt, scale=1.0 / D, bias=eps).then_inc(stats, 1)
                        if first and j == 1 and u == 1:
                            act.dma_start(g_ffpost[:], bcast(norm_ff_post[0])).then_inc(g2_landed, 16)
                        if 1 <= j <= 4 and u == 1:
                            if first and j == 1:
                                act.wait_ge(turned, T_F)
                            else:
                                act.wait_ge(hid_lo_ready, j - 1 + q * 4)
                            copy_hidden(q, j - 1)
                        if 1 <= j <= 4 and u == 4:
                            keep_hidden(q, j - 1)
                        if last and j >= 5 and u == 2:
                            for b in range(BLOCKS):
                                square_f(j - 5, b)
                        if last and j == 7 and u == 3:
                            act.activation(ss3t, rstd1, ACT.Sqrt)
                        if not (last and j == 7 and u + LEAD >= UNITS):
                            uu = (u + LEAD) % UNITS
                            split_hi(uu, C_FF + j + (u + LEAD) // UNITS + q * 8)

            def square_f(j, b):
                n = 2 * j + b
                if n:
                    act.wait_ge(f_squared, n)
                act.wait_ge(acc_free, 2 * (C_FF + 4 * 3 + j) + b + 1)
                act.activation(gate_b[:, 0, :], facc[:, b, j * CW:(j + 1) * CW], ACT.Square,
                               accum_out=ss3[:, b * 4 + j:b * 4 + j + 1]).then_inc(f_squared, 1)

            keep_stream(0)
            quarter(0, first=True)
            with act.Fori(1, QUARTERS - 1) as q:
                quarter(q)
            quarter(QUARTERS - 1, last=True)
            for b in range(BLOCKS):
                square_f(3, b)
                act.wait_ge(norm, 6 + b)
                act.activation(rstd3[:, b:b + 1], ss3t[:, b:b + 1], ACT.Sqrt, scale=1.0 / D, bias=eps)\
                   .then_inc(stats, 1)

        @block.vector
        def _(dve):
            seq = [0]

            def link(ins):
                seq[0] += 1
                ins.then_inc(dve_seq, 1)
                dve.wait_ge(dve_seq, seq[0])

            def split_lo(u, count, width=CW):
                dve.wait_ge(hi_ready, count)
                dve.tensor_tensor(w_lo[:, u, :, 0:width], raw[:, u, :, 0:width],
                                  w_hi[:, u, :, 0:width].bitcast(F32), ALU.subtract).then_inc(lo_ready, 1)

            def split_ahead(c8, u):
                split_lo((u + LEAD) % UNITS, c8 + (u + LEAD + 1))

            def keep_lo(n, dst, src, hi, scale=None):
                dve.wait_ge(turned_hi, n + 1)
                if scale is None:
                    dve.tensor_tensor(dst, src, hi.bitcast(F32), ALU.subtract).then_inc(turned_lo, 1)
                else:
                    dve.scalar_tensor_tensor(dst, src, scale, hi.bitcast(F32), ALU.mult, ALU.subtract)\
                       .then_inc(turned_lo, 1)

            dve.memset(eps, EPS).then_inc(eps_set, 1)
            dve.wait_ge(gain_turned, 1)
            dve.tensor_copy(g_col[:], bank[7][:, 0:KT]).then_inc(gain_ready, 1)
            dve.wait_ge(gain_ready, 1)

            def scale_meta():
                dve.wait_ge(meta_turned, 1)
                gains = g_col[:].rearrange("p (k a) -> p k a", a=1).broadcast_to([P, KT, META])
                dve.tensor_tensor(meta_g[:], bank[6][:, 0:KT * META].rearrange("p (k t) -> p k t", k=KT), gains,
                                  ALU.mult).then_inc(meta_scaled, 1)

            def keep_meta_rows():
                dve.wait_ge(meta_hi_ready, 1)
                dve.tensor_tensor(u_hi[:, :, META:2 * META], meta_g[:], u_hi[:, :, 0:META].bitcast(F32),
                                  ALU.subtract).then_inc(meta_lo_ready, 1)

            def keep_x(i):
                dve.wait_ge(turned_hi, i + 1)
                for k in range(2):
                    kt = 2 * i + k
                    last = dve.scalar_tensor_tensor(u_lo[:, kt, :], bank[2 + i % 4][:, k * SEQ:(k + 1) * SEQ],
                                                    g_col[:, kt:kt + 1], u_hi[:, kt, 2 * META:].bitcast(F32),
                                                    ALU.mult, ALU.subtract)
                last.then_inc(turned_lo, 1)

            for step, i in START_ORDER:
                if step == "x":
                    keep_x(2 * i)
                    keep_x(2 * i + 1)
                else:
                    split_lo(i, i + 1, 256)
                if (step, i) == ("x", 0):
                    scale_meta()
                if (step, i) == ("w", 0):
                    keep_meta_rows()

            dve.wait_ge(xm_twice, 16)
            for u in range(UNITS - LEAD, UNITS):
                j = u - UNITS + LEAD
                if j < 4:
                    cols = slice(j * CW, (j + 1) * CW)
                    link(dve.tensor_tensor_reduce(rows_m[:], xm[:, cols], xm[:, cols], 1.0, 0.0, ALU.mult,
                                                  ALU.add, ss1[0:32, j:j + 1]))
                else:
                    dve.tensor_reduce(ssm, ss1[0:32, 0:4], AX.X, ALU.add)
                split_ahead(0, u)
            dve.wait_ge(table_ready, 1)
            for w in range(2):
                last = dve.tensor_copy(rows[0:HA + HB, w, 0:TAB], bank[(4, 6)[w]][0:HA + HB, 0:TAB])
            last.then_inc(table_copied, 1)
            dve.wait_ge(stats, 8)
            dve.tensor_reduce(ssx, ss3[:].rearrange("p (b j) -> p b j", b=BLOCKS), AX.X, ALU.add)\
               .then_inc(norm, 1)
            dve.wait_ge(small_landed, 7 * 16)
            for i in range(2):
                last = dve.tensor_tensor_reduce(lam_v[:, 2 * i, :], lam_v[:, 2 * i, :], lam_v[:, 2 * i + 1, :],
                                                1.0, 0.0, ALU.mult, ALU.add, lam_dot[:, i:i + 1])
            last.then_inc(norm, 1)
            dve.wait_ge(stats, 10)
            link(dve.reciprocal(rstd, rstd))
            link(dve.reciprocal(rstdm, rstdm))
            dve.tensor_scalar(rstd8, rstd, DHA ** -0.5, None, ALU.mult).then_inc(norm, 1)
            dve.wait_ge(stats, 11)
            link(dve.scalar_tensor_tensor(neg_lam, lam_exp[:, 1:2], LAM_INIT, lam_exp[:, 0:1], ALU.subtract,
                                          ALU.subtract))
            link(dve.tensor_scalar(dcol[:], dcol[:], 1.0 - LAM_INIT, None, ALU.mult))

            def keep_turned(kind, i):
                n = TURN_NO[(kind, i)]
                dve.wait_ge(proj_turned, n + 1)
                g2 = [S0[:].rearrange("p (k t) -> p k t", k=2), TB[:].rearrange("p (k t) -> p k t", k=2)]
                if kind == "kvb":
                    dve.tensor_copy(kbT[:, :, 1 + META:], g2[0])
                    dve.tensor_copy(kbT[:, :, 1:1 + META],
                                    S1[:, 0:2 * META].rearrange("p (k t) -> p k t", k=2))
                    last = dve.tensor_copy(vb_m[:], S1[0:META, 64:64 + P])
                elif kind == "va":
                    last = dve.tensor_copy(va_m[:, i * CW:(i + 1) * CW], TB[0:META, :])
                else:
                    dst, off = {"qb": (qbT, 0), "qa": (qaT, 0), "ka": (kaT, META)}[kind]
                    if kind == "ka":
                        dve.tensor_copy(kaT[:, 4 * i:4 * i + 4, 0:META],
                                        S1[:, 0:4 * META].rearrange("p (k t) -> p k t", k=4))
                    for g in range(2):
                        k0 = 4 * i + 2 * g
                        last = dve.tensor_copy(dst[:, k0:k0 + 2, off:off + SEQ], g2[g])
                last.then_inc(proj_kept, 1)

            def reverse(v, lo, n):
                return v[:, lo + n - 1:(lo - 1 if lo else None):-1]

            def job_max(j):
                windowed = j < HB // 2
                s0 = 1 if windowed else 0
                n0 = P + META + s0
                slot = j % 2
                dve.wait_ge(scores_ready, j + 1)
                if windowed:
                    dve.wait_ge(bias_landed[slot], 64 * (j // 2 + 1))
                    dve.wait_ge(sink_set, j + 1)
                else:
                    dve.wait_ge(bias_landed[slot], 64 * 4 + 16 * ((j - 8) // 2 + 1))
                for e, S in enumerate((S0, S1)):
                    for q, (a, n) in enumerate(((0, n0), (n0, n0 + P))):
                        bv = bias[:, slot, e if windowed else 0, :]
                        lo = a if windowed else 0
                        last = dve.tensor_tensor_reduce(t[:, e, a:a + n], S[:, a:a + n], reverse(bv, lo, n), 1.0,
                                                        -3.0e38, ALU.add, ALU.max,
                                                        mx[:, 2 * e + q:2 * e + q + 1])
                link(last)
                dve.tensor_scalar(nmx, mx, -1.0, None, ALU.mult).then_inc(max_ready, 1)

            def job_combine(j):
                dve.wait_ge(exp_done, j + 1)
                if j < HB // 2:
                    dve.reciprocal(rs, sums).then_inc(probs_ready, 1)
                    return
                link(dve.reciprocal(rs, sums))
                link(dve.scalar_tensor_tensor(cc, sums[:, 0:2], neg_lam, rs[:, 2:4], ALU.mult, ALU.mult))
                n0 = P + META
                for q, (a, n) in enumerate(((0, n0), (n0, n0 + P))):
                    last = dve.scalar_tensor_tensor(t[:, 0, a:a + n], t[:, 1, a:a + n], cc[:, q:q + 1],
                                                    t[:, 0, a:a + n], ALU.mult, ALU.add)
                last.then_inc(probs_ready, 1)

            def job_keep_meta_probs(j):
                dve.wait_ge(probs_turned, j + 1)
                if j < HB // 2:
                    dve.tensor_copy(pTm[:, :, P:2 * P], S1[0:META, 0:2 * P].rearrange("p (e t) -> p e t", e=2))\
                       .then_inc(pTm_kept, 1)
                else:
                    dve.tensor_copy(pTm[:, 0, P:2 * P], MB[0:META, 0:P]).then_inc(pTm_kept, 1)

            def job_keep_out(j):
                dve.wait_ge(o_ready, j + 1)
                if j < HB // 2:
                    c0 = HA * P + j * P
                    dst = y[:, :, c0:c0 + P].rearrange("p q (e d) -> p q e d", e=2)
                    src = S1[:, 2 * P:4 * P].rearrange("p (q e d) -> p q e d", q=2, e=2)
                    r = rs.rearrange("p (e q a) -> p q e a", e=2, a=1).broadcast_to([P, 2, 2, DHB])
                else:
                    h = j - HB // 2
                    dst = y[:, :, h * P:(h + 1) * P]
                    src = MB[:, P:3 * P].rearrange("p (q d) -> p q d", q=2)
                    r = rs[:, 0:2].rearrange("p (q a) -> p q a", a=1).broadcast_to([P, 2, P])
                dve.tensor_tensor(dst, src, r, ALU.mult).then_inc(o_kept, 1)

            def attention(tau):
                for j in range(JOBS):
                    if tau == START[j] + 5:
                        job_keep_out(j)
                    if tau == START[j] + 1:
                        job_max(j)
                    if tau == START[j] + 2:
                        job_combine(j)
                    if tau == START[j] + 4:
                        job_keep_meta_probs(j)
                if tau - 1 in TURN_AT:
                    keep_turned(*TURN_AT[tau - 1])

            for c in range(1, C_MIX):
                for u in range(UNITS):
                    attention(8 * c + u)
                    split_ahead(8 * c, u)

            def keep_y(i):
                g = (i + 4) % 8
                keep_lo(T_Y + i, y_lo[:, 2 * g:2 * g + 2, :],
                        bank[4 + i % 2][:].rearrange("p (k t) -> p k t", k=2), y_hi[:, 2 * g:2 * g + 2, :],
                        dcol[:] if g < 4 else None)

            def mix_b(n):
                dve.wait_ge(used, 8 * (C_MIX + 1) + 4 + n * 16)
                dve.wait_ge(acc_free, 2 * (C_MIX + 1) + n * 4)
                for b in range(BLOCKS):
                    dve.tensor_tensor(gate_b[:, b, :], bank[b][:], gate_b[:, b, :], ALU.mult)\
                       .then_inc(acc_free, 1)

            def mix_a(n):
                dve.wait_ge(used, 8 * (C_MIX + 2) + n * 16)
                dve.wait_ge(gates_ready, 2 + n * 2)
                for b in range(BLOCKS):
                    dve.tensor_tensor(rows[:, b, :], bank[6 + b][:], ga[:, b, bass.ds(n * CW, CW)], ALU.mult)\
                       .then_inc(mix_part, 1)
                for b in range(BLOCKS):
                    dve.wait_ge(mix_part, n * 2 + b + 1)
                    dve.tensor_tensor(rows[:, b, :], rows[:, b, :], gate_b[:, b, :], ALU.add)\
                       .then_inc(mix_ready, 1)

            def keep_mix(n):
                for g in range(2):
                    sl = bass.ds(4 * n + 2 * g, 2)
                    keep_lo(T_M + 2 * n + g, m_lo[:, sl, :], bank[4 + g][:].rearrange("p (k t) -> p k t", k=2),
                            m_hi[:, sl, :])

            def mix_pair(n, first):
                c8 = 8 * C_MIX + n * 16
                for u in range(UNITS):
                    if first:
                        attention(8 * C_MIX + u)
                        if u == 3:
                            dve.wait_ge(stats, 12)
                            link(dve.reciprocal(rstdy, rstdy))
                            for b in range(BLOCKS):
                                v = y[:, b, 0:HA * P].rearrange("p (h d) -> p h d", h=HA)
                                r = rstdy[:, b * HA:(b + 1) * HA].rearrange("p (h a) -> p h a", a=1)\
                                    .broadcast_to([P, HA, P])
                                dve.tensor_tensor(v, v, r, ALU.mult).then_inc(y_scaled, 1)
                        if u >= 1:
                            keep_y(u - 1)
                    else:
                        if u == 1:
                            mix_a(n - 1)
                        if u == 4:
                            keep_mix(n - 1)
                    split_ahead(c8, u)
                for u in range(UNITS):
                    if first and u == 0:
                        keep_y(7)
                    if u == 5:
                        mix_b(n)
                    split_ahead(c8 + 8, u)

            mix_pair(0, True)
            with dve.Fori(1, N_MIX) as n:
                mix_pair(n, False)

            def keep_out(j):
                ps = [bank[2 * ((C_OUT + j) % 2) + b] for b in range(BLOCKS)]
                cols = slice(j * CW, (j + 1) * CW)
                for b in range(BLOCKS):
                    dve.wait_ge(o_squared, 2 * j + b + 1)
                    dve.tensor_tensor(og[:, b, cols], ps[b][:], g_post[:, cols], ALU.mult).then_inc(acc_free, 1)

            for j in range(4):
                for u in range(UNITS):
                    if j == 0 and u == 1:
                        mix_a(N_MIX - 1)
                    if j == 0 and u == 4:
                        keep_mix(N_MIX - 1)
                    if j >= 1 and u == 1:
                        if j == 1:
                            dve.wait_ge(g_post_landed, 16)
                        keep_out(j - 1)
                    split_ahead(8 * (C_OUT + j), u)
            dve.wait_ge(o_squared, 8)
            dve.tensor_reduce(ss1t, ss1.rearrange("p (b j) -> p b j", b=BLOCKS), AX.X, ALU.add).then_inc(norm, 1)
            dve.wait_ge(acc_free, 2 * (C_FF - 1))
            dve.wait_ge(stats, 13)
            link(dve.reciprocal(rstd1, rstd1))

            def new_stream(j):
                cols = slice(j * CW, (j + 1) * CW)
                dst = (rows, gate_b)[j % 2]
                for b in range(BLOCKS):
                    dve.scalar_tensor_tensor(h2[:, b, cols], og[:, b, cols], rstd1[:, b:b + 1], h2[:, b, cols],
                                             ALU.mult, ALU.add).then_inc(hg_part, 1)
                if j >= 2:
                    dve.wait_ge(turned, T_H + 2 * (j - 1))
                for b in range(BLOCKS):
                    dve.wait_ge(hg_part, 2 * j + b + 1)
                    dve.tensor_tensor(dst[:, b, :], h2[:, b, cols], g_ffpre[:, cols], ALU.mult)\
                       .then_inc(hg_ready, 1)

            def keep_stream(j):
                for g in range(2):
                    sl = slice(4 * j + 2 * g, 4 * j + 2 * g + 2)
                    keep_lo(T_H + 2 * j + g, f_hl[:, sl, SEQ:],
                            bank[4 + 2 * (j % 2) + g][:].rearrange("p (k t) -> p k t", k=2), f_hl[:, sl, 0:SEQ])

            def activate_hidden(q, j):
                for g in range(4):
                    dve.wait_ge(hid_copied, 4 * j + g + 1 + q * 16)
                    dve.tensor_tensor(hid_rows[:, g, :], hid_rows[:, g, :], bank[4 * (j % 2) + g][:, SEQ:],
                                      ALU.add).then_inc(hid_summed, 1)
                dve.wait_ge(hid_summed, 4 * (j + 1) + q * 16)
                dve.scalar_tensor_tensor(hid_rows, hid_rows, 0.0, hid_rows, ALU.max, ALU.mult)\
                   .then_inc(hid_ready, 1)

            def keep_hidden(q, j):
                dve.wait_ge(hid_hi_ready, j + 1 + q * 4)
                tiles = slice(4 * j, 4 * j + 4)
                dve.tensor_tensor(hid_lo[:, tiles, :], hid_rows, hid_hi[:, tiles, :].bitcast(F32),
                                  ALU.subtract).then_inc(hid_lo_ready, 1)

            def gain_f(j, b):
                cols = slice(j * CW, (j + 1) * CW)
                dve.wait_ge(f_squared, 2 * j + b + 1)
                dve.tensor_tensor(facc[:, b, cols], facc[:, b, cols], g_ffpost[:, cols], ALU.mult)\
                   .then_inc(f_gained, 1)

            def add_ff2(q, j):
                dve.wait_ge(facc_zero, 1)
                dve.wait_ge(used, 8 * (C_FF + 4 + j + 1) + q * 64)
                for b in range(BLOCKS):
                    add_rows(j, b)

            def add_rows(j, b):
                cols = slice(j * CW, (j + 1) * CW)
                dve.scalar_tensor_tensor(facc[:, b, cols], bank[4 * (j % 2) + b][:], rstd2[:, b:b + 1],
                                         facc[:, b, cols], ALU.mult, ALU.add).then_inc(acc_free, 1)

            def quarter(q, first=False, last=False):
                for j in range(8):
                    for u in range(UNITS):
                        if first and j == 0:
                            if u in (0, 2, 4):
                                new_stream(u // 2 + 1)
                            if u in (1, 3, 5):
                                keep_stream((u + 1) // 2)
                            if u == 7:
                                dve.wait_ge(stats, 13 + 8)
                                dve.tensor_reduce(ss2t, ss2[:].rearrange("p (b j) -> p b j", b=BLOCKS), AX.X,
                                                  ALU.add).then_inc(norm, 1)
                        if first and j == 1 and u == 0:
                            dve.wait_ge(stats, 14 + 8)
                            link(dve.reciprocal(rstd2, rstd2))
                            link(dve.tensor_tensor(rstd2, rstd2, rstd2, ALU.mult))
                        if 1 <= j <= 4:
                            if u == 2:
                                activate_hidden(q, j - 1)
                            if u == 5:
                                keep_hidden(q, j - 1)
                        if j >= 5 and u == 1:
                            add_ff2(q, j - 5)
                        if last and j >= 5 and u == 4:
                            for b in range(BLOCKS):
                                gain_f(j - 5, b)
                        if not (last and j == 7 and u + LEAD >= UNITS):
                            split_lo((u + LEAD) % UNITS, 8 * (C_FF + j) + u + LEAD + 1 + q * 64)
                if not last:
                    add_ff2(q, 3)

            dve.wait_ge(tail_landed, 16 * 5)
            new_stream(0)
            keep_out(3)
            dve.wait_ge(acc_free, 2 * C_FF)
            keep_stream(0)
            quarter(0, first=True)
            dve.wait_ge(g2_landed, 16)
            with dve.Fori(1, QUARTERS - 1) as q:
                quarter(q)
            quarter(QUARTERS - 1, last=True)
            cols = slice(3 * CW, 4 * CW)
            for b in range(BLOCKS):
                dve.wait_ge(last_rows, b + 1)
                add_rows(3, b)
                dve.wait_ge(f_squared, 6 + b + 1)
                dve.tensor_reduce(ss3t[:, b:b + 1], ss3[:, 4 * b:4 * b + 4], AX.X, ALU.add).then_inc(norm, 1)
                gain_f(3, b)
                dve.wait_ge(stats, 15 + 8 + b)
                link(dve.reciprocal(rstd3[:, b:b + 1], rstd3[:, b:b + 1]))
                dve.wait_ge(f_gained, 7 + b)
                for j in range(4):
                    cj = slice(j * CW, (j + 1) * CW)
                    dve.scalar_tensor_tensor(facc[:, b, cj], facc[:, b, cj], rstd3[:, b:b + 1], h2[:, b, cj],
                                             ALU.mult, ALU.add).then_inc(out_ready, 1)

        @block.tensor
        def _(pe):
            def turn4(dst, pieces):
                for i, v in enumerate(pieces):
                    ins = pe.transpose(dst[:, i * P:(i + 1) * P], v, ident[:])
                return ins

            def multiply(c8, u, hi_of, lo_of, ps, width=CW, first=0, last=UNITS - 1, meta=None,
                         blocks=range(BLOCKS)):
                pe.wait_ge(lo_ready, c8 + u + 1)
                for k in range(UK):
                    kt = (u - first) * UK + k
                    a, z = u == first and k == 0, u == last and k == UK - 1
                    wh, wl = w_hi[:, u, k, 0:width], w_lo[:, u, k, 0:width]
                    for b in blocks:
                        pe.matmul(ps[b][:, 0:width], hi_of(kt, b), wh, start=a, stop=False)
                        pe.matmul(ps[b][:, 0:width], hi_of(kt, b), wl, start=False, stop=False)
                        ins = pe.matmul(ps[b][:, 0:width], lo_of(kt, b), wh, start=False, stop=z)
                if meta is not None:
                    if u == 0 and meta == 0:
                        pe.wait_ge(meta_lo_ready, 1)
                    if u == 0 and meta > 0:
                        pe.wait_ge(meta_ready, meta)
                    for k in range(UK):
                        kt = u * UK + k
                        a, z = kt == 0, kt == KT - 1
                        pe.matmul(MB[:, 0:width], u_hi[:, kt, 0:P], w_hi[:, u, k, 0:width], start=a, stop=False)
                        ins = pe.matmul(MB[:, 0:width], u_hi[:, kt, 0:P], w_lo[:, u, k, 0:width], start=False,
                                        stop=z)
                return ins.then_inc(used, 1) if blocks == range(BLOCKS) else ins

            def rows_of(t_hi, t_lo, off=0):
                return (lambda kt, b: t_hi[:, kt, off + b * P:off + (b + 1) * P],
                        lambda kt, b: t_lo[:, kt, b * P:(b + 1) * P])

            pe.wait_ge(consts_landed, 32)
            pe.transpose(bank[7][:, 0:KT], g_rows[:], ident[0:KT, 0:KT]).then_inc(gain_turned, 1)

            def turn_meta():
                pe.wait_ge(xm_landed, 16)
                for kt in range(KT):
                    ins = pe.transpose(bank[6][:, kt * META:(kt + 1) * META], xm[0:META, kt * P:(kt + 1) * P],
                                       ident[0:META, 0:META])
                ins.then_inc(meta_turned, 1)

            def turn_x(j):
                pe.wait_ge(x_landed[j], 16)
                for i in (2 * j, 2 * j + 1):
                    if i >= 4:
                        pe.wait_ge(turned_lo, i - 3)
                    turn4(bank[2 + i % 4], [xs[:, b, (2 * i + k) * P:(2 * i + k + 1) * P]
                                            for k in range(2) for b in range(BLOCKS)]).then_inc(turned, 1)

            def bias_table():
                pe.wait_ge(rel_landed, 32)
                pe.wait_ge(turned_lo, 7)
                for w in range(2):
                    ins = pe.matmul(bank[(4, 6)[w]][0:HA + HB, 0:TAB], relx[:], buck[:, w, :], start=True,
                                    stop=True)
                ins.then_inc(table_ready, 1)

            def turn_rows(kind, i):
                n = TURN_NO[(kind, i)]
                if n:
                    pe.wait_ge(proj_kept, n)
                if kind == "kvb":
                    pe.wait_ge(acc_free, 2)
                    pe.wait_ge(meta_ready, 1)
                    pe.wait_ge(small_landed, 7 * 16)
                    for g in range(HKV):
                        for b in range(BLOCKS):
                            pe.transpose(S0[:, (2 * g + b) * P:(2 * g + b + 1) * P],
                                         rows[:, b, g * P:(g + 1) * P], ident[:])
                    for g in range(HKV):
                        pe.matmul(S1[:, g * META:(g + 1) * META], rows_m[:, g * P:(g + 1) * P], fold_m[:],
                                  start=True, stop=True)
                    pe.matmul(S1[0:META, 64:64 + P], fold_m[:], rows_m[:, 2 * P:3 * P], start=True, stop=True)\
                      .then_inc(proj_turned, 1)
                    return
                if kind == "va":
                    pe.wait_ge(meta_ready, {0: 3, 1: 5}[i])
                    pe.matmul(TB[0:META, :], fold_m[:], rows_m[:], start=True, stop=True).then_inc(proj_turned, 1)
                    return
                c = {"qb": C_QB + i, "qa": C_A + 3 * i, "ka": C_A + 3 * i + 1}[kind]
                pe.wait_ge(acc_free, 2 * (c + 1))
                if kind == "ka":
                    pe.wait_ge(meta_ready, {0: 2, 1: 4}[i])
                    pe.wait_ge(o_kept, {0: 4, 1: 8}[i])
                    for g in range(4):
                        pe.matmul(S1[:, g * META:(g + 1) * META], rows_m[:, g * P:(g + 1) * P], fold_m[:],
                                  start=True, stop=True)
                for g, dst in enumerate((S0, TB)):
                    ins = turn4(dst, [rows[:, b, (2 * g + k) * P:(2 * g + k + 1) * P]
                                      for k in range(2) for b in range(BLOCKS)])
                ins.then_inc(proj_turned, 1)

            def kept_by(tau):
                return sum(1 for at in TURN_AT if at < tau)

            def job_scores(j):
                windowed = j < HB // 2
                s0 = 1 if windowed else 0
                n0 = P + META + s0
                pe.wait_ge(proj_kept, kept_by(START[j]))
                if windowed:
                    pe.wait_ge(kb_zero, 1)
                    if j:
                        pe.wait_ge(o_kept, j)
                elif j == HB // 2:
                    pe.wait_ge(o_kept, j)
                for e, S in enumerate((S0, S1)):
                    rows_ = slice(64 * e, 64 * e + 64)
                    q, k = (qbT[rows_, j, :], kbT[rows_, j // 4, :]) if windowed else \
                           (qaT[rows_, j - 8, :], kaT[rows_, j - 8, :])
                    pe.matmul(S[:, 0:n0], q[:, 0:P], k[:, 0:n0], start=True, stop=True)
                    ins = pe.matmul(S[:, n0:2 * n0 + P], q[:, P:2 * P], k[:, 0:n0 + P], start=True, stop=True)
                ins.then_inc(scores_ready, 1)

            def job_turn(j):
                windowed = j < HB // 2
                s0 = 1 if windowed else 0
                n0 = P + META + s0
                pe.wait_ge(probs_ready, j + 1)
                pe.wait_ge(proj_kept, kept_by(START[j] + 3))
                if j > HB // 2:
                    pe.wait_ge(o_kept, j)
                if j == HB // 2:
                    pe.wait_ge(meta_ready, 5)
                for e, dst in enumerate((TB, S0) if windowed else (TB,)):
                    r0 = s0 + META
                    pe.transpose(dst[:, 0:P], t[:, e, r0:r0 + P], ident[:])
                    pe.transpose(dst[:, P:2 * P], t[:, e, n0 + r0:n0 + r0 + P], ident[:])
                    pe.transpose(dst[:, 2 * P:3 * P], t[:, e, n0 + r0 + P:n0 + r0 + 2 * P], ident[:])
                    pe.transpose(dst[0:META, 3 * P:4 * P], t[:, e, s0:r0], ident[:])
                    m1 = S1[0:META, e * P:(e + 1) * P] if windowed else MB[0:META, 0:P]
                    ins = pe.transpose(m1, t[:, e, n0 + s0:n0 + r0], ident[:])
                ins.then_inc(probs_turned, 1)

            def job_values(j):
                windowed = j < HB // 2
                pe.wait_ge(pT_kept, j + 1)
                pe.wait_ge(pTm_kept, j + 1)
                for e in range(2 if windowed else 1):
                    if windowed:
                        col, dv, g = slice((j // 4) * DHB, (j // 4 + 1) * DHB), DHB, None
                        vm, vr = vb_m[:, col], [vb[:, b, col] for b in range(BLOCKS)]
                    else:
                        h = j - HB // 2
                        col = slice(h * P, (h + 1) * P)
                        vm, vr = va_m[:, col], [va[:, b, col] for b in range(BLOCKS)]
                    for q in range(2):
                        o = S1[:, 2 * P + q * P + e * DHB:2 * P + q * P + (e + 1) * DHB] if windowed else \
                            MB[:, P + q * P:P + (q + 1) * P]
                        pe.matmul(o, pTm[:, e, q * P:(q + 1) * P], vm, start=True, stop=False)
                        ins = pe.matmul(o, pT[:, e, q * P:(q + 1) * P], vr[0], start=False, stop=q == 0)
                        if q == 1:
                            ins = pe.matmul(o, pT[:, e, 2 * P:3 * P], vr[1], start=False, stop=True)
                ins.then_inc(o_ready, 1)

            def attention(tau):
                for j in range(JOBS):
                    if tau == START[j] + 4:
                        job_values(j)
                for j in range(JOBS):
                    if tau == START[j] + 3:
                        job_turn(j)
                if tau in TURN_AT:
                    turn_rows(*TURN_AT[tau])
                for j in range(JOBS):
                    if tau == START[j]:
                        job_scores(j)

            x_hi, x_lo = rows_of(u_hi, u_lo, 2 * META)
            turn_x(0)
            turn_meta()
            turn_x(1)
            for c in range(C_MIX):
                ps = [bank[2 * (c % 2) + b] for b in range(BLOCKS)]
                if c >= 2:
                    pe.wait_ge(acc_free, 2 * (c - 1))
                for u in range(UNITS):
                    if c == 0:
                        pe.wait_ge(turned_lo, u + 1)
                    multiply(8 * c, u, x_hi, x_lo, ps, 256 if c == 0 else CW,
                             meta=META_WAIT.get(c))
                    if c == 0 and u < 2:
                        turn_x(u + 2)
                    if c == 0 and u == 6:
                        bias_table()
                    attention(8 * c + u)

            def turn_y(i):
                g = (i + 4) % 8
                if i >= 2:
                    pe.wait_ge(turned_lo, T_Y + i - 1)
                if i == 4:
                    pe.wait_ge(y_scaled, 2)
                turn4(bank[4 + i % 2], [y[:, b, (2 * g + k) * P:(2 * g + k + 1) * P]
                                        for k in range(2) for b in range(BLOCKS)]).then_inc(turned, 1)

            def turn_mix(n):
                pe.wait_ge(mix_ready, 2 + n * 2)
                pe.wait_ge(turned_lo, T_M + n * 2)
                for g in range(2):
                    turn4(bank[4 + g], [rows[:, b, (2 * g + k) * P:(2 * g + k + 1) * P]
                                        for k in range(2) for b in range(BLOCKS)]).then_inc(turned, 1)

            yb_hi, yb_lo = rows_of(y_hi, y_lo)

            def mix_pair(n, first):
                c8 = 8 * C_MIX + n * 16
                pe.wait_ge(acc_free, 2 * (C_MIX - 1) + n * 4)
                for u in range(UNITS):
                    multiply(c8, u, x_hi, x_lo, [bank[2], bank[3]])
                    if first:
                        attention(8 * C_MIX + u)
                        turn_y(u)
                    elif u == 3:
                        turn_mix(n - 1)
                pe.wait_ge(acc_free, 2 * C_MIX + n * 4)
                for u in range(4):
                    if first and u == 0:
                        pe.wait_ge(turned_lo, T_Y + 4)
                    multiply(c8 + 8, u, lambda kt, b: yb_hi(kt + 8, b), lambda kt, b: yb_lo(kt + 8, b),
                             [bank[0], bank[1]], last=3)
                if first:
                    pe.wait_ge(turned_lo, T_Y + 8)
                else:
                    pe.wait_ge(mix_ready, n * 2)
                for u in range(4, UNITS):
                    multiply(c8 + 8, u, yb_hi, yb_lo, [bank[6], bank[7]], first=4)

            mix_pair(0, True)
            with pe.Fori(1, N_MIX) as n:
                mix_pair(n, False)

            m = rows_of(m_hi, m_lo)
            for j in range(4):
                c = C_OUT + j
                pe.wait_ge(acc_free, 2 * (c - 1))
                for u in range(UNITS):
                    if j == 0 and u == 6:
                        pe.wait_ge(turned_lo, T_H)
                    multiply(8 * c, u, *m, [bank[2 * (c % 2) + b] for b in range(BLOCKS)])
                    if j == 0 and u == 3:
                        turn_mix(N_MIX - 1)

            def turn_stream(j):
                pe.wait_ge(hg_ready, 2 * (j + 1))
                if j >= 2:
                    pe.wait_ge(turned_lo, T_H + 2 * (j - 1))
                src = (rows, gate_b)[j % 2]
                for g in range(2):
                    turn4(bank[4 + 2 * (j % 2) + g], [src[:, b, (2 * g + k) * P:(2 * g + k + 1) * P]
                                                      for k in range(2) for b in range(BLOCKS)])\
                        .then_inc(turned, 1)

            hid = rows_of(hid_hi, hid_lo)

            def multiply_hidden(c8, u, acc):
                pe.wait_ge(lo_ready, c8 + u + 1)
                for k in range(UK):
                    kt = u * UK + k
                    for g in range(4):
                        cols = slice(g * P, (g + 1) * P)
                        both = lambda: pe.matmul(acc[g][:], w_hi[:, u, k, cols], f_hl[:, kt, :],
                                                 start=kt == 0, stop=kt == KT - 1)
                        low = lambda: pe.matmul(acc[g][:, 0:SEQ], w_lo[:, u, k, cols], f_hl[:, kt, 0:SEQ],
                                                start=False, stop=False)
                        for product in ((low, both) if kt == KT - 1 else (both, low)):
                            ins = product()
                ins.then_inc(used, 1)

            def quarter(q, first=False, last=False):
                for j in range(8):
                    c = C_FF + j
                    acc = [bank[4 * (j % 2) + g] for g in range(4)]
                    if first and j == 0:
                        pe.wait_ge(acc_free, 2 * C_FF)
                    elif first and j == 1:
                        pe.wait_ge(turned_lo, T_F)
                    elif j < 2:
                        pe.wait_ge(acc_free, 2 * C_FF + 2 * (j - 1) + q * 8)
                    elif j < 6:
                        pe.wait_ge(hid_summed, 4 * (j - 1) + q * 16)
                    else:
                        pe.wait_ge(acc_free, 2 * C_FF + 2 * (j - 5) + q * 8)
                    if last and j == 7:
                        for b in range(BLOCKS):
                            for u in range(UNITS):
                                ins = multiply(8 * c + q * 64, u, *hid, acc, blocks=(b,))
                            ins.then_inc(last_rows, 1)
                        continue
                    if j == 4:
                        pe.wait_ge(hid_lo_ready, 3 + q * 4)
                    for u in range(UNITS):
                        if j == 4 and u == 6:
                            pe.wait_ge(hid_lo_ready, 4 + q * 4)
                        if first and j == 0:
                            pe.wait_ge(turned_lo, T_H + u + 1)
                        if j < 4:
                            multiply_hidden(8 * c + q * 64, u, acc)
                        else:
                            multiply(8 * c + q * 64, u, *hid, acc)
                        if first and j == 0 and u in (0, 2, 4):
                            turn_stream(u // 2 + 1)

            turn_stream(0)
            quarter(0, first=True)
            with pe.Fori(1, QUARTERS - 1) as q:
                quarter(q)
            quarter(QUARTERS - 1, last=True)


def has_meta(c):
    return c == 0 or (C_A <= c < C_GA and (c - C_A) % 3 > 0)


META_WAIT = {0: 0, 4: 1, 5: 2, 7: 3, 8: 4}

_INS = ["x", "meta_tokens", "rel_bias", "w_in", "w_branch_a", "w_branch_b", "w_out", "lambda_q1", "lambda_k1",
        "lambda_q2", "lambda_k2", "diff_norm", "sinks", "norm_attn_pre", "norm_attn_post", "w_ff1", "w_ff2",
        "norm_ff_pre", "norm_ff_post"]


def kernel(**inputs):
    import concourse.bacc as bacc
    from concourse.bass_utils import run_bass_kernel_spmd

    nc = bacc.Bacc("TRN2", target_bir_lowering=False, num_devices=1)
    given = {name: np.ascontiguousarray(inputs[name]) for name in _INS}
    given["identity"] = np.eye(P, dtype=np.float32)
    given["fold"] = np.concatenate([np.eye(META, dtype=np.float32)] * 2)
    given["buckets"] = bucket_table()
    arrays, args = {}, []
    for name, a in given.items():
        arrays[f"in_{name}"] = a
        args.append(nc.dram_tensor(f"in_{name}", a.shape, mybir.dt.from_np(a.dtype), kind="ExternalInput").ap())
    args.append(nc.dram_tensor("out_h", (1, SEQ, D), F32, kind="ExternalOutput").ap())
    hybrid_block(nc, *args)
    r = run_bass_kernel_spmd(nc, [arrays], core_ids=[0])
    return r.results[0]["out_h"]
```
